# Optimizing a Trainium2 kernel written in Bass

```python
import math
import jax, jax.numpy as jnp
from jax import lax
import numpy as np

D_MODEL = 1024
BATCH = 1
SEQ = 2048
DEPTH = 1

EPS = 1e-6
NEG_INF = -1e30

ATTN_HEADS = 8
ATTN_KV_HEADS = 2
ATTN_HEAD_DIM = 64
ATTN_WIDTH = ATTN_HEADS * ATTN_HEAD_DIM
ATTN_KV_WIDTH = ATTN_KV_HEADS * ATTN_HEAD_DIM
WINDOW = 128
BLOCK = 128

NUM_BUCKETS = 32
MAX_DISTANCE = 128

GLA_HEADS = 4
GLA_KEY_DIM = 64
GLA_VALUE_DIM = 128
GLA_KEY_WIDTH = GLA_HEADS * GLA_KEY_DIM
GLA_WIDTH = GLA_HEADS * GLA_VALUE_DIM
GLA_GATE_RANK = 16
GLA_GATE_NORMALIZER = 16.0
GLA_CHUNK = 64

MIX_WIDTH = ATTN_WIDTH + GLA_WIDTH
SPLIT_SIZES = (ATTN_WIDTH, ATTN_KV_WIDTH, ATTN_KV_WIDTH, ATTN_WIDTH,
               GLA_KEY_WIDTH, GLA_KEY_WIDTH, GLA_WIDTH, GLA_WIDTH, GLA_GATE_RANK)
N_IN = sum(SPLIT_SIZES)

kernel_name = "hybrid_swa_sink_gla_parallel_heads"

def rmsnorm(x, gain):
    xf = x.astype(jnp.float32)
    y = xf * lax.rsqrt(jnp.mean(xf * xf, axis=-1, keepdims=True) + EPS) * gain.astype(jnp.float32)
    return y.astype(x.dtype)

def t5_causal_bucket(dist):
    n = jnp.maximum(dist, 0)
    max_exact = NUM_BUCKETS // 2
    nf = jnp.maximum(n, 1).astype(jnp.float32)
    large = max_exact + (jnp.log(nf / max_exact) / math.log(MAX_DISTANCE / max_exact)
                         * (NUM_BUCKETS - max_exact)).astype(jnp.int32)
    large = jnp.minimum(large, NUM_BUCKETS - 1)
    return jnp.where(n < max_exact, n, large)

def sliding_window_attention(q, k, v, sinks, rel_bias):
    B, S = q.shape[0], q.shape[1]
    nb = S // BLOCK
    G = ATTN_HEADS // ATTN_KV_HEADS
    qb = q.reshape(B, nb, BLOCK, ATTN_KV_HEADS, G, ATTN_HEAD_DIM)
    kb = k.reshape(B, nb, BLOCK, ATTN_KV_HEADS, ATTN_HEAD_DIM)
    vb = v.reshape(B, nb, BLOCK, ATTN_KV_HEADS, ATTN_HEAD_DIM)

    def with_prev(t):
        prev = jnp.concatenate([jnp.zeros_like(t[:, :1]), t[:, :-1]], axis=1)
        return jnp.concatenate([prev, t], axis=2)

    kw, vw = with_prev(kb), with_prev(vb)
    scale = ATTN_HEAD_DIM ** -0.5
    scores = jnp.einsum("bnqkgd,bnckd->bnkgqc", qb, kw).astype(jnp.float32) * scale

    qi = jnp.arange(BLOCK)
    ci = jnp.arange(2 * BLOCK)
    dist = qi[:, None] + BLOCK - ci[None, :]
    in_window = (dist >= 0) & (dist < WINDOW)
    bias = rel_bias.astype(jnp.float32)[t5_causal_bucket(dist)]
    bias = bias.transpose(2, 0, 1).reshape(ATTN_KV_HEADS, G, BLOCK, 2 * BLOCK)
    key_exists = (jnp.arange(nb)[:, None] > 0) | (ci[None, :] >= BLOCK)
    mask = in_window[None, :, :] & key_exists[:, None, :]

    scores = jnp.where(mask[None, :, None, None], scores + bias[None, None], NEG_INF)
    sink = sinks.astype(jnp.float32).reshape(ATTN_KV_HEADS, G)[None, None, :, :, None, None]
    m = jnp.maximum(jnp.max(scores, axis=-1, keepdims=True), sink)
    p = jnp.exp(scores - m)
    probs = p / (jnp.sum(p, axis=-1, keepdims=True) + jnp.exp(sink - m))
    out = jnp.einsum("bnkgqc,bnckd->bnqkgd", probs.astype(v.dtype), vw)
    return out.reshape(B, S, ATTN_WIDTH)

def gla_chunked(q, k, v, g):
    B, S = q.shape[0], q.shape[1]
    nc = S // GLA_CHUNK
    f32 = jnp.float32

    def rs(t):
        return t.astype(f32).reshape(B, nc, GLA_CHUNK, GLA_HEADS, t.shape[-1])

    qc = rs(q) * (GLA_KEY_DIM ** -0.5)
    kc, vc, gc = rs(k), rs(v), rs(g)
    b = jnp.cumsum(gc, axis=2)
    b_last = b[:, :, -1]
    q_dec = qc * jnp.exp(b)
    k_dec = kc * jnp.exp(-b)
    k_to_end = kc * jnp.exp(b_last[:, :, None] - b)

    causal = jnp.tril(jnp.ones((GLA_CHUNK, GLA_CHUNK), dtype=bool))
    A = jnp.where(causal, jnp.einsum("bnihd,bnjhd->bnhij", q_dec, k_dec), 0.0)
    o_intra = jnp.einsum("bnhij,bnjhv->bnihv", A, vc)
    kv_upd = jnp.einsum("bnjhd,bnjhv->bnhdv", k_to_end, vc)

    def step(state, inp):
        q_d, decay, upd = inp
        o = jnp.einsum("bihd,bhdv->bihv", q_d, state)
        return decay[..., None] * state + upd, o

    init = jnp.zeros((B, GLA_HEADS, GLA_KEY_DIM, GLA_VALUE_DIM), f32)
    xs = (jnp.moveaxis(q_dec, 1, 0), jnp.moveaxis(jnp.exp(b_last), 1, 0), jnp.moveaxis(kv_upd, 1, 0))
    _, o_inter = lax.scan(step, init, xs)
    o = o_intra + jnp.moveaxis(o_inter, 0, 1)
    return o.reshape(B, S, GLA_HEADS, GLA_VALUE_DIM).astype(q.dtype)

def hybrid_layer(x, norm_gain, w_in, w_gate_up, b_gate, rel_bias, sinks, gla_norm_gain, w_out):
    B, S = x.shape[0], x.shape[1]
    h = rmsnorm(x, norm_gain)
    proj = h @ w_in
    idx = list(np.cumsum(SPLIT_SIZES)[:-1])
    q_a, k_a, v_a, z_a, q_g, k_g, v_g, z_g, r_g = jnp.split(proj, idx, axis=-1)

    attn = sliding_window_attention(
        q_a.reshape(B, S, ATTN_HEADS, ATTN_HEAD_DIM),
        k_a.reshape(B, S, ATTN_KV_HEADS, ATTN_HEAD_DIM),
        v_a.reshape(B, S, ATTN_KV_HEADS, ATTN_HEAD_DIM),
        sinks, rel_bias)
    attn = attn * jax.nn.silu(z_a)

    gk = jax.nn.log_sigmoid((r_g @ w_gate_up + b_gate).astype(jnp.float32)) / GLA_GATE_NORMALIZER
    o = gla_chunked(
        q_g.reshape(B, S, GLA_HEADS, GLA_KEY_DIM),
        k_g.reshape(B, S, GLA_HEADS, GLA_KEY_DIM),
        v_g.reshape(B, S, GLA_HEADS, GLA_VALUE_DIM),
        gk.reshape(B, S, GLA_HEADS, GLA_KEY_DIM))
    gla = rmsnorm(o, gla_norm_gain).reshape(B, S, GLA_WIDTH) * jax.nn.silu(z_g)

    y = jnp.concatenate([attn, gla], axis=-1) @ w_out
    return x + y

def setup_inputs(seed: int = 0) -> dict:
    key = jax.random.key(seed)
    ks = jax.random.split(key, 11)
    nrm = jax.random.normal
    return {
        "x": nrm(ks[0], (BATCH, SEQ, D_MODEL), jnp.float32),
        "norm_gain": 1.0 + 0.01 * nrm(ks[1], (DEPTH, D_MODEL), jnp.float32),
        "w_in": nrm(ks[2], (DEPTH, D_MODEL, N_IN), jnp.float32) * D_MODEL ** -0.5,
        "w_gate_up": nrm(ks[3], (DEPTH, GLA_GATE_RANK, GLA_KEY_WIDTH), jnp.float32) * GLA_GATE_RANK ** -0.5,
        "b_gate": 0.1 * nrm(ks[4], (DEPTH, GLA_KEY_WIDTH), jnp.float32),
        "rel_bias": 0.1 * nrm(ks[5], (NUM_BUCKETS, ATTN_HEADS), jnp.float32),
        "sinks": 0.5 * nrm(ks[6], (DEPTH, ATTN_HEADS), jnp.float32),
        "gla_norm_gain": 1.0 + 0.01 * nrm(ks[7], (DEPTH, GLA_VALUE_DIM), jnp.float32),
        "w_out": nrm(ks[8], (DEPTH, MIX_WIDTH, D_MODEL), jnp.float32) * MIX_WIDTH ** -0.5,
        "final_norm_gain": 1.0 + 0.01 * nrm(ks[9], (D_MODEL,), jnp.float32),
    }

def reference(x, norm_gain, w_in, w_gate_up, b_gate, rel_bias, sinks, gla_norm_gain, w_out, final_norm_gain):
    for l in range(DEPTH):
        x = hybrid_layer(x, norm_gain[l], w_in[l], w_gate_up[l], b_gate[l], rel_bias,
                         sinks[l], gla_norm_gain[l], w_out[l])
    return rmsnorm(x, final_norm_gain)


_drawn_inputs = setup_inputs


def setup_inputs(seed=0):
    import zlib

    import numpy as np

    out = dict(_drawn_inputs(seed))
    spreads = {}
    factors = {'norm_gain': 6.528,
     'b_gate': 3.321,
     'rel_bias': 8.0,
     'sinks': 8.0,
     'gla_norm_gain': 8.0,
     'final_norm_gain': 5.703}
    for name, (base, spread) in spreads.items():
        noise = np.random.default_rng([zlib.crc32(name.encode()), seed]).standard_normal(out[name].shape)
        drawn = base * np.exp(spread * noise) if base else spread * noise
        out[name] = __import__('jax').numpy.asarray(drawn.astype(out[name].dtype))
    for name, factor in factors.items():
        out[name] = (out[name] * factor).astype(out[name].dtype)
    return out
```

```python
from contextlib import ExitStack

import numpy as np

import concourse.bass as bass
from concourse import mybir

F32 = mybir.dt.float32
F32R = mybir.dt.float32r
BF16 = mybir.dt.bfloat16
ALU = mybir.AluOpType
ACT = mybir.ActivationFunctionType

P = 128
D = 1024
S = 2048
T = S // P
KT = D // P
EPS = 1e-6
NEG = -1e30

AH, AKV, AD = 8, 2, 64
AG = AH // AKV
AW, AKW = AH * AD, AKV * AD
NUM_BUCKETS, MAX_DISTANCE, WINDOW = 32, 128, 128
GH, GK, GV, GR, GC = 4, 64, 128, 16, 64
GKW, GW = GH * GK, GH * GV
GATE_NORM = 16.0

C_Q, C_KV = 0, AW
C_ZA = C_KV + 2 * AKW
C_QK = C_ZA + AW
C_V = C_QK + 2 * GKW
C_ZG = C_V + GW
C_R = C_ZG + GW
N_IN = C_R + GR

NA = C_QK + GW
A_Q, A_KV, A_ZA, A_ZG = C_Q, C_KV, C_ZA, C_QK
NB = 2 * GKW + GW
B_QK, B_V = 0, 2 * GKW
HALF = KT // 2


def bucket(n):
    exact = NUM_BUCKETS // 2
    if n < exact:
        return n
    large = exact + int(np.log(n / exact) / np.log(MAX_DISTANCE / exact) * (NUM_BUCKETS - exact))
    return min(large, NUM_BUCKETS - 1)


def bucket_runs():
    runs = []
    for j in range(P, 2 * P):
        b = bucket(2 * P - 1 - j)
        if runs and runs[-1][2] == b:
            runs[-1][1] = j + 1
        else:
            runs.append([j, j + 1, b])
    return runs


def a_filled(t, k):
    return 9 * t + (k - 3)


def a_bank(k):
    return (k + 2) % 3


def a_prior(t, k):
    return 3 * t + (k - 4) // 3


def b_short(t, k):
    return isinstance(t, int) and (t == T or (t == T - 1 and k == 5))


def b_filled(t, k):
    return 6 * t + (k - (3 if b_short(t, k) else 1))


def b_prior(t, k):
    return 3 * t + (k // 2 - (2 if b_short(t, k) else 1))


def acc_use(t, g):
    if isinstance(t, int) and t == 0:
        return g
    if isinstance(t, int) and t == T:
        return 4 * t - 4 + g
    return 4 * t + (g - 2)


def acc_prior(t, g):
    if isinstance(t, int) and t == 0:
        return 0
    if isinstance(t, int) and t == T:
        return 2 * t + (g - 4) // 2
    return 2 * t + (g // 2 - 1)


def steps(eng, body):
    body(0, 0)
    body(1, 1)
    with eng.Fori(2, T - 2, 2) as t:
        body(t, 0)
        body(t + 1, 1)
    for t in range(T - 2, T + 1):
        body(t, t % 2)


def hybrid_block(nc, x, norm_gain, w_in, w_gate_up, b_gate, rel_bias, sinks, gla_norm_gain, w_out,
                 final_norm_gain, out):
    x_t = x.rearrange("o (t p) d -> (o t) p d", p=P)
    out_t = out.rearrange("o (t p) d -> (o t) p d", p=P)
    w_in_k = w_in.rearrange("l (k p) n -> (l k) p n", p=P)
    w_out_k = w_out.rearrange("l (k p) n -> (l k) p n", p=P)
    mix_dram = nc.dram_tensor("mix_scratch", (T, P, D), F32).ap()
    line_dram = nc.dram_tensor("bias_lines", (AH, P, 3 * P), F32)

    with ExitStack() as ctx:
        def sb(name, shape, dt=F32):
            return ctx.enter_context(nc.sbuf_tensor(name, shape, dt))

        def sem(name):
            return ctx.enter_context(nc.semaphore(name))

        weights = sb("weights", [P, 2 * KT * (NB + D)], F32R)
        wa = weights[:, 0:2 * KT * NA].rearrange("p (s k n) -> p s k n", s=2, k=KT)
        wb = weights[:, 0:2 * KT * NB].rearrange("p (s k n) -> p s k n", s=2, k=KT)
        wo = weights[:, 2 * KT * NB:2 * KT * (NB + D)].rearrange("p (s k n) -> p s k n", s=2, k=KT)
        xb = sb("xb", [P, 2, D])
        ht = sb("ht", [P, 2, 2, KT, P], F32R)
        junk = sb("junk", [P, D], BF16)
        ez = sb("ez", [P, 4, AW])
        stage = ez[:, :, :].rearrange("p (s c) n -> p s (c n)", s=2)
        stage_r = sb("stage_r", [P, KT, GR])
        ident = sb("ident", [P, P])
        gain_col = sb("gain_col", [P, KT])
        gla_gain_col = sb("gla_gain_col", [P, 1])
        half = sb("half", [P, AH])
        ss = sb("ss", [P, 2])
        ms = sb("ms", [P, 2])
        rstd = sb("rstd", [P, 2])
        ident_r = sb("ident_r", [P, P], F32R)
        w_r = sb("w_r", [P, KT, 2 * GR], F32R)
        r_t = sb("r_t", [2 * GR + 1, P])
        w_up = sb("w_up", [2 * GR + 1, GKW])
        scan_mask = sb("scan_mask", [P, 2 * P])
        sink = sb("sink", [P, AH])
        mx = sb("mx", [P, AH])
        nmx = sb("nmx", [P, AH])
        sinkd = sb("sinkd", [P, AH])
        esink = sb("esink", [P, AH])
        psum_row = sb("psum_row", [P, AH])
        den = sb("den", [P, AH])
        rden = sb("rden", [P, AH])
        rel_t = sb("rel_t", [AH, NUM_BUCKETS])
        line = sb("line", [AH, 3 * P])
        zline = sb("zline", [AH, P])

        x_loaded = [sem(f"x_loaded{i}") for i in range(2)]
        const_loaded = sem("const_loaded")
        gain_loaded = sem("gain_loaded")
        const_set = sem("const_set")
        held = sem("held")
        ident_set = sem("ident_set")
        line_set = sem("line_set")
        line_stored = sem("line_stored")
        bias_loaded = sem("bias_loaded")
        raw_loaded = [sem(f"raw_loaded{i}") for i in range(2)]
        raw_r_loaded = sem("raw_r_loaded")
        w_hi = sem("w_hi")
        w_lo = sem("w_lo")
        ss_ready = sem("ss_ready")
        ms_ready = sem("ms_ready")
        rstd_ready = sem("rstd_ready")
        h_ready = sem("h_ready")
        h_hi = sem("h_hi")

        def settle(eng):
            eng.wait_ge(ident_set, 2)

        def hold(eng):
            eng.sem_inc(held, 1)

        def square_x(act, n, slot, loads):
            act.wait_ge(x_loaded[slot], loads)
            nc.scalar.activation(junk[:], xb[:, slot, :], ACT.Square,
                                 accum_out=ss[:, slot:slot + 1]).then_inc(ss_ready, 1)

        def rstd_x(pool, n, slot):
            pool.wait_ge(ss_ready, n + 1)
            hold(pool)
            nc.gpsimd.tensor_scalar(ms[:, slot:slot + 1], ss[:, slot:slot + 1], 1.0 / D, EPS,
                                    ALU.mult, ALU.add).then_inc(ms_ready, 1)
            pool.wait_ge(ms_ready, n + 1)
            nc.gpsimd.tensor_tensor(rstd[:, slot:slot + 1], ms[:, slot:slot + 1], half[:, 0:1],
                                    ALU.pow).then_inc(rstd_ready, 1)

        def scale_x(dve, n, slot):
            dve.wait_ge(rstd_ready, n + 1)
            nc.vector.tensor_scalar(xb[:, slot, :], xb[:, slot, :], rstd[:, slot:slot + 1], None,
                                    ALU.mult).then_inc(h_ready, 1)

        with ExitStack() as pa:
            def sba(name, shape, dt=F32):
                return pa.enter_context(nc.sbuf_tensor(name, shape, dt))

            def banka(name):
                return pa.enter_context(nc.psum_tensor(name, [P, 512], F32))

            probs = sba("probs", [P, AH, 2 * P])
            probs_t = sba("probs_t", [P, AH, 2, P])
            raw_a = [probs[:, :, :].rearrange("p h c -> p (h c)")[:, 0:NA],
                     probs_t[:, :, :, :].rearrange("p h s c -> p (h s c)")[:, 0:NA]]
            bias = sba("bias", [P, AH, 2 * P])
            q2 = sba("q2", [P, AH, 2 * AD], F32R)
            q2t = sba("q2t", [P, AH, P], F32R)
            k2 = sba("k2", [P, 2, AKV, 2, AD], F32R)
            k2t = sba("k2t", [P, 2, 2, AKV, P], F32R)
            va = sba("va", [P, 2, AKV, AD])
            gate_a = sba("gate_a", [P, 2, AW])
            gate_g = sba("gate_g", [P, 2, GW])
            mixa = sba("mixa", [P, 2, AW])
            acc = [banka(f"acc{i}") for i in range(2)]
            tp = [banka(f"tp{i}") for i in range(3)]
            sc = [banka(f"sc{i}") for i in range(2)]
            oa = banka("oa")

            acc_filled = sem("acc_filled")
            acc_drained = [sem(f"acc_drained{i}") for i in range(2)]
            tp_filled = sem("tp_filled")
            tp_drained = [sem(f"tp_drained{i}") for i in range(3)]
            sc_filled = sem("sc_filled")
            sc_drained = [sem(f"sc_drained{i}") for i in range(2)]
            oa_filled = sem("oa_filled")
            q_hi = sem("q_hi")
            k_hi = sem("k_hi")
            nmx_ready = sem("nmx_ready")
            sinkd_ready = sem("sinkd_ready")
            exp_ready = sem("exp_ready")
            esink_ready = sem("esink_ready")
            den_ready = sem("den_ready")
            rden_ready = sem("rden_ready")
            e_ready = sem("e_ready")
            e1_ready = sem("e1_ready")
            rec_ready = sem("rec_ready")
            gate_ready = sem("gate_ready")
            gate_scaled = sem("gate_scaled")
            mixa_ready = sem("mixa_ready")
            mixa_stored = sem("mixa_stored")
            gate_stored = sem("gate_stored")

            runs = bucket_runs()

            def a_data(eng, t, k):
                eng.wait_ge(tp_drained[a_bank(k)], a_prior(t, k) + 1)

            with nc.Block() as block:
                @block.sync
                def _(sp):
                    sp.dma_start(xb[:, 0, :], x_t[0]).then_inc(x_loaded[0], 16)
                    sp.dma_start(gain_col[:], norm_gain.rearrange("l (k p) -> (l p) k", p=P),
                                 allow_slow_non_contiguous=True).then_inc(gain_loaded, 16)
                    for k in range(KT):
                        if k >= 2:
                            sp.wait_ge(w_lo, k - 1)
                        raw = raw_a[k % 2]
                        sp.dma_start(raw[:, 0:C_QK], w_in_k[k, :, 0:C_QK]).then_inc(raw_loaded[k % 2], 16)
                        sp.dma_start(raw[:, A_ZG:NA], w_in_k[k, :, C_ZG:C_R]).then_inc(raw_loaded[k % 2], 16)
                        if k == 0:
                            sp.dma_start(xb[:, 1, :], x_t[1]).then_inc(x_loaded[1], 16)
                        if k == 1:
                            sp.dma_start(rel_t[:], rel_bias.rearrange("b h -> h b"),
                                         allow_slow_non_contiguous=True).then_inc(const_loaded, 16)
                            sp.dma_start(sink[:], sinks[0].partition_broadcast(P)).then_inc(const_loaded, 16)
                            sp.dma_start(gla_gain_col[:], gla_norm_gain.rearrange("l v -> v l"),
                                         allow_slow_non_contiguous=True).then_inc(const_loaded, 16)
                            sp.dma_start(w_up[0:GR, :], w_gate_up[0]).then_inc(const_loaded, 16)
                            sp.dma_start(w_up[GR:2 * GR, :], w_gate_up[0]).then_inc(const_loaded, 16)
                            sp.dma_start(w_up[2 * GR:, :], b_gate).then_inc(const_loaded, 16)
                    sp.wait_ge(line_set, 2 + len(runs))
                    sp.dma_start(line_dram.ap(), line[:].unsqueeze(1).to_broadcast((AH, P, 3 * P))).then_inc(line_stored, 16)
                    sp.wait_ge(line_stored, 16)
                    for h in range(AH):
                        sp.dma_start(bias[:, h, :],
                                     bass.AP(line_dram, h * P * 3 * P + P - 1, [[3 * P - 1, P], [1, 2 * P]]))\
                          .then_inc(bias_loaded, 16)
                    sp.wait_ge(tp_filled, 2)
                    sp.dma_start(xb[:, 0, :], x_t[2]).then_inc(x_loaded[0], 16)

                    def step(t, p, index):
                        settle(sp)
                        sp.wait_ge(gate_ready, 2 * t + 2)
                        sp.dma_start(mix_dram[t, :, AW:D], gate_g[:, p, :]).then_inc(gate_stored, 16)
                        if not (isinstance(t, int) and t == 0):
                            settle(sp)
                            sp.wait_ge(mixa_ready, t)
                            sp.dma_start(mix_dram[t - 1, :, 0:AW], mixa[:, 1 - p, :]).then_inc(mixa_stored, 16)
                        settle(sp)
                        sp.wait_ge(tp_filled, a_filled(t, 7))
                        sp.dma_start(xb[:, 1 - p, :], x_t[index]).then_inc(x_loaded[1 - p], 16)

                    step(0, 0, 3)
                    step(1, 1, 4)
                    with sp.Fori(2, T - 4, 2) as t:
                        step(t, 0, t + 3)
                        step(t + 1, 1, t + 4)
                    for t in range(T - 4, T):
                        step(t, t % 2, (t + 3) % T)
                    settle(sp)
                    sp.wait_ge(mixa_ready, T)
                    sp.dma_start(mix_dram[T - 1, :, 0:AW], mixa[:, 1, :]).then_inc(mixa_stored, 16)

                @block.gpsimd
                def _(pool):
                    nc.gpsimd.memset(half[:], -0.5).then_inc(const_set, 1)
                    nc.gpsimd.memset(ident[:], 0.0).then_inc(ident_set, 1)
                    pool.wait_ge(ident_set, 1)
                    nc.gpsimd.affine_select(out=ident[:], in_=ident[:], compare_op=ALU.not_equal,
                                            fill=1.0, base=0, pattern=[[-1, P]],
                                            channel_multiplier=1).then_inc(ident_set, 1)
                    nc.gpsimd.memset(r_t[:], 1.0).then_inc(const_set, 1)
                    nc.gpsimd.memset(scan_mask[:], 1.0).then_inc(const_set, 1)
                    pool.wait_ge(const_set, 3)
                    nc.gpsimd.memset(scan_mask[:].rearrange("p (c j) -> p c j", j=GC)[:, :, 0:1], 0.0)\
                        .then_inc(const_set, 1)
                    rstd_x(pool, 0, 0)

                    def add_one(t, j):
                        pool.wait_ge(e_ready, 2 * t + (j + 1))
                        hold(pool)
                        nc.gpsimd.tensor_scalar(ez[:, j, :], ez[:, j, :], 1.0, None, ALU.add)\
                            .then_inc(e1_ready, 1)

                    def step(t, p):
                        first = isinstance(t, int) and t == 0
                        tail = isinstance(t, int) and t == T
                        if not tail:
                            rstd_x(pool, t + 1, 1 - p)
                            add_one(t, 0)
                            pool.wait_ge(rec_ready, 4 * t + 2)
                            pool.wait_ge(acc_drained[0], 2 * t + 1)
                            if not (isinstance(t, int) and t < 2):
                                pool.wait_ge(mixa_ready, t - 1)
                            nc.gpsimd.tensor_tensor(gate_a[:, p, :], ez[:, 2, :], ez[:, 0, :], ALU.mult)\
                                .then_inc(gate_ready, 1)
                            add_one(t, 1)
                        if not first:
                            pool.wait_ge(rden_ready, t)
                            if tail:
                                pool.wait_ge(gate_ready, 2 * t - 1)
                            g = gate_a[:, 1 - p, :].rearrange("p (h d) -> p h d", d=AD)
                            nc.gpsimd.tensor_tensor(g, g, rden[:, :].unsqueeze(2).to_broadcast((P, AH, AD)),
                                                    ALU.mult).then_inc(gate_scaled, 1)
                        if not tail:
                            pool.wait_ge(rec_ready, 4 * t + 4)
                            pool.wait_ge(acc_drained[1], 2 * t + 1)
                            if not (isinstance(t, int) and t < 2):
                                pool.wait_ge(gate_stored, 16 * t - 16)
                            nc.gpsimd.tensor_tensor(gate_g[:, p, :], ez[:, 3, :], ez[:, 1, :], ALU.mult)\
                                .then_inc(gate_ready, 1)

                    steps(pool, step)

                @block.scalar
                def _(act):
                    nc.scalar.preload_act_table_set("natural_log_exp_and_others")
                    square_x(act, 0, 0, 16)
                    act.wait_ge(gain_loaded, 16)

                    def h_part_hi(t, k, slot):
                        act.wait_ge(tp_filled, a_filled(t, 6 + k))
                        nc.scalar.activation(ht[:, slot, 0, HALF * k:HALF * k + HALF, :],
                                             tp[a_bank(6 + k)][:, :].rearrange("p (k c) -> p k c", c=P),
                                             ACT.Copy).then_inc(h_hi, 1)

                    for k in range(KT):
                        act.wait_ge(raw_loaded[k % 2], 32 * (k // 2 + 1))
                        nc.scalar.activation(wa[:, 0, k, :], raw_a[k % 2], ACT.Copy,
                                             scale=gain_col[:, k:k + 1]).then_inc(w_hi, 1)
                        if k == 0:
                            for j in range(2):
                                act.wait_ge(tp_filled, j + 1)
                                nc.scalar.activation(ht[:, 0, 0, HALF * j:HALF * j + HALF, :],
                                                     tp[j][:, :].rearrange("p (k c) -> p k c", c=P),
                                                     ACT.Copy).then_inc(h_hi, 1)

                    def step(t, p):
                        first = isinstance(t, int) and t == 0
                        second = isinstance(t, int) and t == 1
                        tail = isinstance(t, int) and t == T
                        lo = P if second else 0
                        if not tail:
                            square_x(act, t + 1, 1 - p, 8 * t + (16 if p == 0 else 24))
                        if not first:
                            act.wait_ge(tp_filled, a_filled(t, 0))
                            nc.scalar.activation(q2t[:, 0:4, :], tp[a_bank(0)][:, :].rearrange(
                                "p (h c) -> p h c", c=P), ACT.Copy).then_inc(tp_drained[a_bank(0)], 1)

                        def exp_z(j):
                            act.wait_ge(acc_filled, 4 * t + (j + 1))
                            if not first:
                                act.wait_ge(gate_ready, 2 * t + (j - 1))
                            nc.scalar.activation(ez[:, j, :], acc[j][:, :], ACT.Exp, scale=-1.0)\
                                .then_inc(e_ready, 1)
                            nc.scalar.activation(ez[:, 2 + j, :], acc[j][:, :], ACT.Copy)\
                                .then_inc(acc_drained[j], 1)

                        def exps(h0):
                            act.wait_ge(nmx_ready, 2 * t + (h0 // 4 - 1))
                            for h in range(h0, h0 + 4):
                                nc.scalar.activation(probs[:, h, lo:], probs[:, h, lo:], ACT.Exp,
                                                     bias=nmx[:, h:h + 1],
                                                     accum_out=psum_row[:, h:h + 1]).then_inc(exp_ready, 1)

                        def probs_t_out(j):
                            act.wait_ge(tp_filled, a_filled(t, 2 + j))
                            b = a_bank(2 + j)
                            src = tp[b][:, :].rearrange("p (h s c) -> p h s c", h=2, s=2)
                            nc.scalar.activation(probs_t[:, 2 * j:2 * j + 2, lo // P:, :], src[:, :, lo // P:, :],
                                                 ACT.Copy).then_inc(tp_drained[b], 1)

                        if not tail:
                            exp_z(0)
                        if not first:
                            exps(0)
                        if not tail:
                            exp_z(1)
                        if not first:
                            exps(4)
                            act.wait_ge(sinkd_ready, t)
                            nc.scalar.activation(esink[:], sinkd[:], ACT.Exp).then_inc(esink_ready, 1)
                            probs_t_out(0)
                            probs_t_out(2)
                        if not tail:
                            h_part_hi(t, 0, 1 - p)
                            h_part_hi(t, 1, 1 - p)
                            act.wait_ge(tp_filled, a_filled(t, 8))
                            nc.scalar.activation(k2t[:, p, :, :, :], tp[a_bank(8)][:, :].rearrange(
                                "p (s h c) -> p s h c", s=2, h=AKV), ACT.Copy)\
                                .then_inc(tp_drained[a_bank(8)], 1)
                            act.wait_ge(acc_filled, 4 * t + 4)
                            if not first:
                                act.wait_ge(tp_filled, a_filled(t, 1))
                            nc.scalar.activation(q2[:, :, 0:AD], acc[1][:, :].rearrange(
                                "p (h d) -> p h d", d=AD), ACT.Copy, scale=AD ** -0.5).then_inc(q_hi, 1)

                    steps(act, step)

                @block.vector
                def _(dve):
                    nc.vector.memset(line[:], NEG).then_inc(line_set, 1)
                    nc.vector.memset(zline[:], 0.0).then_inc(line_set, 1)
                    scale_x(dve, 0, 0)
                    dve.wait_ge(ident_set, 2)
                    nc.vector.tensor_copy(ident_r[:], ident[:]).then_inc(ident_set, 1)
                    dve.wait_ge(const_loaded, 96)
                    dve.wait_ge(line_set, 2)
                    for a, b, k in runs:
                        nc.vector.tensor_scalar(line[:, a:b], zline[:, 0:b - a], rel_t[:, k:k + 1], None,
                                                ALU.add).then_inc(line_set, 1)
                    for k in range(KT):
                        dve.wait_ge(w_hi, k + 1)
                        nc.vector.scalar_tensor_tensor(out=wa[:, 1, k, :], in0=raw_a[k % 2],
                                                       scalar=gain_col[:, k:k + 1],
                                                       in1=wa[:, 0, k, :].bitcast(F32),
                                                       op0=ALU.mult, op1=ALU.subtract).then_inc(w_lo, 1)
                        if k == 0:
                            for j in range(2):
                                dve.wait_ge(h_hi, j + 1)
                                nc.vector.tensor_tensor(ht[:, 0, 1, HALF * j:HALF * j + HALF, :],
                                                        tp[j][:, :].rearrange("p (k c) -> p k c", c=P),
                                                        ht[:, 0, 0, HALF * j:HALF * j + HALF, :].bitcast(F32),
                                                        ALU.subtract).then_inc(tp_drained[j], 1)
                    def step(t, p):
                        first = isinstance(t, int) and t == 0
                        second = isinstance(t, int) and t == 1
                        tail = isinstance(t, int) and t == T
                        lo = P if second else 0

                        def bias_max(h0):
                            for h in range(h0, h0 + 4):
                                dve.wait_ge(sc_filled, 4 * t + (h // 2 - 3))
                                hold(dve)
                                b = (h // 2) % 2
                                src = sc[b][:, (h % 2) * 2 * P + lo:(h % 2) * 2 * P + 2 * P]
                                last = nc.vector.tensor_tensor_reduce(
                                    probs[:, h, lo:], src, bias[:, h, lo:], 1.0, sink[:, h:h + 1],
                                    ALU.add, ALU.max, mx[:, h:h + 1])
                                if h % 2:
                                    last.then_inc(sc_drained[b], 1)
                            dve.wait_ge(sc_drained[0], 2 * t + (h0 // 4 - 1))
                            dve.wait_ge(sc_drained[1], 2 * t + (h0 // 4 - 1))
                            nc.vector.tensor_scalar(nmx[:, h0:h0 + 4], mx[:, h0:h0 + 4], -1.0, None,
                                                    ALU.mult).then_inc(nmx_ready, 1)

                        def recip(j, c):
                            dve.wait_ge(e1_ready, 2 * t + (j + 1))
                            nc.vector.reciprocal(ez[:, j, 256 * c:256 * c + 256],
                                                 ez[:, j, 256 * c:256 * c + 256]).then_inc(rec_ready, 1)

                        def probs_t_out(j):
                            dve.wait_ge(tp_filled, a_filled(t, 2 + j))
                            b = a_bank(2 + j)
                            src = tp[b][:, :].rearrange("p (h s c) -> p h s c", h=2, s=2)
                            nc.vector.tensor_copy(probs_t[:, 2 * j:2 * j + 2, lo // P:, :],
                                                  src[:, :, lo // P:, :]).then_inc(tp_drained[b], 1)

                        if not tail:
                            scale_x(dve, t + 1, 1 - p)
                        if not first:
                            dve.wait_ge(tp_filled, a_filled(t, 1))
                            nc.vector.tensor_copy(q2t[:, 4:8, :], tp[a_bank(1)][:, :].rearrange(
                                "p (h c) -> p h c", c=P)).then_inc(tp_drained[a_bank(1)], 1)
                            if second:
                                dve.wait_ge(bias_loaded, 16 * AH)
                            bias_max(0)
                        if not tail:
                            recip(0, 0)
                        if not first:
                            bias_max(4)
                            dve.wait_ge(nmx_ready, 2 * t)
                            nc.vector.tensor_tensor(sinkd[:], sink[:], nmx[:], ALU.add).then_inc(sinkd_ready, 1)
                        if not tail:
                            recip(0, 1)
                        if not first:
                            probs_t_out(1)
                            dve.wait_ge(exp_ready, 8 * t)
                            dve.wait_ge(esink_ready, t)
                            nc.vector.tensor_tensor(den[:], psum_row[:], esink[:], ALU.add).then_inc(den_ready, 1)
                            dve.wait_ge(den_ready, t)
                            nc.vector.reciprocal(rden[:], den[:]).then_inc(rden_ready, 1)
                            probs_t_out(3)
                        if not tail:
                            recip(1, 0)
                            dve.wait_ge(acc_filled, 4 * t + 3)
                            if not first:
                                dve.wait_ge(tp_filled, a_filled(t, 0))
                            kin = acc[0][:, 0:AKW].rearrange("p (h d) -> p h d", d=AD)
                            for c in range(2):
                                last = nc.vector.tensor_copy(k2[:, 0, :, c, :], kin)
                                last.then_inc(k_hi, 1)
                            dve.wait_ge(k_hi, 2 * t + 2)
                            for c in range(2):
                                nc.vector.tensor_tensor(k2[:, 1, :, c, :], kin, k2[:, 0, :, 0, :].bitcast(F32),
                                                        ALU.subtract)
                            if not first:
                                dve.wait_ge(oa_filled, t)
                            nc.vector.tensor_copy(va[:, p, :, :], acc[0][:, AKW:2 * AKW].rearrange(
                                "p (h d) -> p h d", d=AD)).then_inc(acc_drained[0], 1)
                        if not first:
                            dve.wait_ge(oa_filled, t)
                            dve.wait_ge(gate_scaled, t)
                            if not second:
                                dve.wait_ge(mixa_stored, 16 * t - 16)
                            nc.vector.tensor_tensor(mixa[:, 1 - p, :], oa[:, :], gate_a[:, 1 - p, :],
                                                    ALU.mult).then_inc(mixa_ready, 1)
                        if not tail:
                            for k in range(2):
                                dve.wait_ge(h_hi, 2 * t + (3 + k))
                                nc.vector.tensor_tensor(
                                    ht[:, 1 - p, 1, HALF * k:HALF * k + HALF, :],
                                    tp[a_bank(6 + k)][:, :].rearrange("p (k c) -> p k c", c=P),
                                    ht[:, 1 - p, 0, HALF * k:HALF * k + HALF, :].bitcast(F32),
                                    ALU.subtract).then_inc(tp_drained[a_bank(6 + k)], 1)
                            recip(1, 1)
                            dve.wait_ge(q_hi, t + 1)
                            nc.vector.scalar_tensor_tensor(
                                out=q2[:, :, AD:2 * AD],
                                in0=acc[1][:, :].rearrange("p (h d) -> p h d", d=AD), scalar=AD ** -0.5,
                                in1=q2[:, :, 0:AD].bitcast(F32), op0=ALU.mult, op1=ALU.subtract)\
                                .then_inc(acc_drained[1], 1)

                    steps(dve, step)

                @block.tensor
                def _(pe):
                    def h_transposes(t, k, slot, xslot):
                        b = a_bank(6 + k)
                        for c in range(4):
                            kt = HALF * k + c
                            last = nc.tensor.transpose(tp[b][:, c * P:(c + 1) * P],
                                                       xb[:, xslot, kt * P:(kt + 1) * P], ident[:])
                        last.then_inc(tp_filled, 1)

                    pe.wait_ge(ident_set, 2)
                    pe.wait_ge(h_ready, 1)
                    for j in range(2):
                        for c in range(4):
                            kt = HALF * j + c
                            last = nc.tensor.transpose(tp[j][:, c * P:(c + 1) * P],
                                                       xb[:, 0, kt * P:(kt + 1) * P], ident[:])
                        last.then_inc(tp_filled, 1)

                    def step(t, p):
                        first = isinstance(t, int) and t == 0
                        second = isinstance(t, int) and t == 1
                        tail = isinstance(t, int) and t == T

                        def project(g, col, n, halves):
                            b = g % 2
                            if 0 in halves and not (first and g < 2):
                                pe.wait_ge(acc_drained[b], 2 * t + g // 2)
                            for half_ in halves:
                                for kt in range(HALF * half_, HALF * half_ + HALF):
                                    if first and g == 0:
                                        pe.wait_ge(w_lo, kt + 1)
                                    hi, lo = ht[:, p, 0, kt, :], ht[:, p, 1, kt, :]
                                    for i, (a, w) in enumerate(((hi, 0), (hi, 1), (lo, 0))):
                                        last = nc.tensor.matmul(acc[b][:, 0:n], a, wa[:, w, kt, col:col + n],
                                                                start=(kt == 0 and i == 0),
                                                                stop=(kt == KT - 1 and i == 2))
                            if 1 in halves:
                                last.then_inc(acc_filled, 1)

                        def q_transposes(k):
                            b = a_bank(k)
                            pe.wait_ge(tp_drained[b], a_prior(t, k))
                            pe.wait_ge(acc_drained[1], 2 * t)
                            for c in range(4):
                                last = nc.tensor.matmul(tp[b][:, c * P:(c + 1) * P],
                                                        q2[:, 4 * k + c, :], ident_r[:], start=True, stop=True)
                            last.then_inc(tp_filled, 1)

                        def scores(h0):
                            a_data(pe, t, h0 // 4)
                            if h0 == 0:
                                a_data(pe, t - 1, 8)
                            for h in range(h0, h0 + 4):
                                b = (h // 2) % 2
                                if h % 2 == 0 and not (second and h0 == 0):
                                    pe.wait_ge(sc_drained[b], 2 * t + (h0 // 4 - 2))
                                for s in range(1 if second else 0, 2):
                                    slot = 1 - p if s else p
                                    for w in range(2):
                                        last = nc.tensor.matmul(
                                            sc[b][:, (h % 2) * 2 * P + s * P:(h % 2) * 2 * P + (s + 1) * P],
                                            q2t[:, h, :], k2t[:, slot, w, h // AG, :],
                                            start=(w == 0), stop=(w == 1))
                                if h % 2:
                                    last.then_inc(sc_filled, 1)

                        def probs_transposes(j):
                            b = a_bank(2 + j)
                            pe.wait_ge(tp_drained[b], a_prior(t, 2 + j))
                            pe.wait_ge(exp_ready, 8 * t + (2 * j - 6))
                            for h in range(2):
                                for s in range(1 if second else 0, 2):
                                    last = nc.tensor.transpose(tp[b][:, (2 * h + s) * P:(2 * h + s + 1) * P],
                                                               probs[:, 2 * j + h, s * P:(s + 1) * P], ident[:])
                            last.then_inc(tp_filled, 1)

                        def attend(h0):
                            if h0 == 0 and not second:
                                pe.wait_ge(mixa_ready, t - 1)
                            if h0 == 0:
                                pe.wait_ge(acc_drained[0], 2 * t)
                            for h in range(h0, h0 + 4):
                                if h % 2 == 0:
                                    a_data(pe, t, 2 + h // 2)
                                for s in range(1 if second else 0, 2):
                                    slot = 1 - p if s else p
                                    last = nc.tensor.matmul(oa[:, h * AD:(h + 1) * AD], probs_t[:, h, s, :],
                                                            va[:, slot, h // AG, :],
                                                            start=(s == (1 if second else 0)), stop=(s == 1))
                            if h0 == 4:
                                last.then_inc(oa_filled, 1)

                        if tail:
                            for k in range(2):
                                q_transposes(k)
                            scores(0)
                            scores(4)
                            for j in range(2):
                                probs_transposes(j)
                            for j in range(2, 4):
                                probs_transposes(j)
                            attend(0)
                            attend(4)
                            return
                        if first:
                            pe.wait_ge(ident_set, 3)
                            pe.wait_ge(tp_drained[0], 1)
                            pe.wait_ge(tp_drained[1], 1)
                        else:
                            for k in range(2):
                                a_data(pe, t - 1, 6 + k)
                        project(0, A_ZA, AW, (0,))
                        if not first:
                            q_transposes(0)
                            q_transposes(1)
                        project(0, A_ZA, AW, (1,))
                        if not first:
                            scores(0)
                        project(1, A_ZG, GW, (0,))
                        if not first:
                            scores(4)
                        project(1, A_ZG, GW, (1,))
                        if not first:
                            probs_transposes(0)
                            probs_transposes(1)
                        project(2, A_KV, 2 * AKW, (0,))
                        if not first:
                            probs_transposes(2)
                            probs_transposes(3)
                            attend(0)
                        project(2, A_KV, 2 * AKW, (1,))
                        if not first:
                            attend(4)
                        pe.wait_ge(h_ready, t + 2)
                        for k in range(2):
                            pe.wait_ge(tp_drained[a_bank(6 + k)], a_prior(t, 6 + k))
                            h_transposes(t, k, 1 - p, 1 - p)
                        project(3, A_Q, AW, (0,))
                        pe.wait_ge(tp_drained[a_bank(8)], a_prior(t, 8))
                        pe.wait_ge(acc_drained[0], 2 * t + 2)
                        for s in range(2):
                            for h in range(AKV):
                                last = nc.tensor.matmul(
                                    tp[a_bank(8)][:, (2 * s + h) * P:(2 * s + h + 1) * P],
                                    k2[:, s, h, :, :].rearrange("p c d -> p (c d)"), ident_r[:],
                                    start=True, stop=True)
                        last.then_inc(tp_filled, 1)
                        project(3, A_Q, AW, (1,))

                    steps(pe, step)

        with ExitStack() as pb:
            def sbb(name, shape, dt=F32):
                return pb.enter_context(nc.sbuf_tensor(name, shape, dt))

            def bankb(name):
                return pb.enter_context(nc.psum_tensor(name, [P, 512], F32))

            yb = sbb("yb", [P, 2, D])
            mix = sbb("mix", [P, D])
            mix_t = sbb("mix_t", [P, 2, KT, P], F32R)
            gain_row = sbb("gain_row", [P, D])
            qk = sbb("qk", [P, 2 * GKW])
            vb = sbb("vb", [P, GW])
            l_b = sbb("l_b", [P, 2 * P])
            ls_b = sbb("ls_b", [P, 2 * P])
            b_b = sbb("b_b", [P, 2, 2, GC])
            bl = sbb("bl", [P, 2, 2, 2])
            e_up = sbb("e_up", [P, 2, P])
            e_dn = sbb("e_dn", [P, 2, P])
            q_dec = sbb("q_dec", [P, 2, P])
            k_dec = sbb("k_dec", [P, 2, P])
            k_tok = sbb("k_tok", [P, 2, P])
            a_t = sbb("a_t", [P, 2, 2, P])
            state = sbb("state", [P, 2, GV])
            state_x = sbb("state_x", [P, 2, GV])
            junk_y = sbb("junk_y", [P, D], BF16)
            junk_g = sbb("junk_g", [P, GH, GV], BF16)
            fsum = sbb("fsum", [P, 2])
            fexp = sbb("fexp", [P, 2])
            ss4 = sbb("ss4", [P, GH])
            ms4 = sbb("ms4", [P, GH])
            rs4 = sbb("rs4", [P, GH])
            ssy = sbb("ssy", [P, 2])
            msy = sbb("msy", [P, 2])
            rsy = sbb("rsy", [P, 2])
            acc = [bankb(f"b_acc{i}") for i in range(2)]
            tp = [bankb(f"b_tp{i}") for i in range(2)]
            rb = bankb("b_r")
            at = [bankb(f"b_at{i}") for i in range(2)]
            ob = bankb("b_o")
            o_b = [ob[:, 0:2 * GV].rearrange("p (j v) -> p j v", v=GV),
                   at[1][:, 256:512].rearrange("p (j v) -> p j v", v=GV)]
            mix_g = mix[:, AW:D].rearrange("p (j o v) -> p o j v", o=2, v=GV)
            u_b = at[0][:, 256:512].rearrange("p (j v) -> p j v", v=GV)

            b_acc_filled = sem("b_acc_filled")
            b_acc_drained = [sem(f"b_acc_drained{i}") for i in range(2)]
            b_tp_filled = sem("b_tp_filled")
            b_tp_drained = [sem(f"b_tp_drained{i}") for i in range(2)]
            r_filled = sem("r_filled")
            rt_copied = sem("rt_copied")
            l_ready = sem("l_ready")
            ls_ready = sem("ls_ready")
            b_scanned = sem("b_scanned")
            bl_ready = sem("bl_ready")
            b_mid = sem("b_mid")
            fsum_ready = sem("fsum_ready")
            fexp_ready = sem("fexp_ready")
            decay_ready = sem("decay_ready")
            qk_dec_ready = sem("qk_dec_ready")
            at_filled = sem("at_filled")
            at_copied = sem("at_copied")
            at_masked = sem("at_masked")
            u_filled = sem("u_filled")
            x_state = sem("x_state")
            state_ready = sem("state_ready")
            o_filled = sem("o_filled")
            ss4_ready = sem("ss4_ready")
            ms4_ready = sem("ms4_ready")
            rs4_ready = sem("rs4_ready")
            mixg_scaled = sem("mixg_scaled")
            mix_ready = sem("mix_ready")
            mix_hi = sem("mix_hi")
            mix_loaded = sem("mix_loaded")
            y_loaded = [sem(f"y_loaded{i}") for i in range(2)]
            ssy_ready = sem("ssy_ready")
            msy_ready = sem("msy_ready")
            rsy_ready = sem("rsy_ready")
            y_scaled = sem("y_scaled")
            out_stored = [sem(f"out_stored{i}") for i in range(2)]
            gain_loaded_b = sem("gain_loaded_b")
            b_set = sem("b_set")

            def pass_a_done(eng):
                eng.wait_ge(mixa_ready, T)
                eng.wait_ge(mixa_stored, 16 * T)
                eng.wait_ge(gate_stored, 16 * T)

            def b_data(eng, t, k):
                eng.wait_ge(b_tp_drained[k % 2], b_prior(t, k) + 1)

            def acc_data(eng, t, g):
                eng.wait_ge(b_acc_drained[g % 2], acc_prior(t, g) + 1)

            def is_t(t, n):
                return isinstance(t, int) and t == n

            with nc.Block() as block:
                @block.sync
                def _(sp):
                    sp.wait_ge(gate_ready, 2 * T)
                    for k in range(2 * KT):
                        if k >= 2:
                            sp.wait_ge(w_lo, KT + k - 1)
                        if k < KT:
                            src = w_in_k[k, :, C_QK:C_ZG]
                        else:
                            src = w_out_k[k - KT]
                        sp.dma_start(stage[:, k % 2, :], src).then_inc(raw_loaded[k % 2], 16)
                        if k == 0:
                            sp.dma_start(stage_r[:], w_in_k[:, :, C_R:N_IN].rearrange("k p n -> p k n"))\
                              .then_inc(raw_r_loaded, 16)
                        if k == 3:
                            pass_a_done(sp)
                            sp.dma_start(mix[:], mix_dram[0]).then_inc(mix_loaded, 16)
                            sp.dma_start(yb[:, 0, :], x_t[0]).then_inc(y_loaded[0], 16)
                            sp.dma_start(gain_row[:], final_norm_gain.partition_broadcast(P))\
                              .then_inc(gain_loaded_b, 16)

                    def step(t, p):
                        if not (isinstance(t, int) and t < 2):
                            settle(sp)
                            sp.wait_ge(y_scaled, t - 1)
                            sp.dma_start(out_t[t - 2], yb[:, p, :]).then_inc(out_stored[p], 16)
                        if is_t(t, T):
                            return
                        if not is_t(t, 0):
                            settle(sp)
                            sp.wait_ge(b_tp_filled, b_filled(t, 1))
                            sp.dma_start(mix[:], mix_dram[t]).then_inc(mix_loaded, 16)
                            if not is_t(t, 1):
                                settle(sp)
                                sp.wait_ge(out_stored[p], 8 * t if p == 0 else 8 * t - 8)
                            sp.dma_start(yb[:, p, :], x_t[t]).then_inc(y_loaded[p], 16)
                        if not (isinstance(t, int) and t > T - 4):
                            settle(sp)
                            sp.wait_ge(b_tp_filled, b_filled(t, 4))
                            sp.dma_start(xb[:, 1 - p, :], x_t[t + 3]).then_inc(x_loaded[1 - p], 16)

                    step(0, 0)
                    step(1, 1)
                    with sp.Fori(2, T - 4, 2) as t:
                        step(t, 0)
                        step(t + 1, 1)
                    for t in range(T - 4, T + 1):
                        step(t, t % 2)
                    settle(sp)
                    sp.wait_ge(y_scaled, T)
                    sp.dma_start(out_t[T - 1], yb[:, (T - 1) % 2, :]).then_inc(out_stored[(T - 1) % 2], 16)
                    for p in range(2):
                        sp.wait_ge(out_stored[p], 8 * T)

                @block.gpsimd
                def _(pool):
                    pass_a_done(pool)
                    nc.gpsimd.memset(state_x[:], 0.0).then_inc(b_set, 1)
                    nc.gpsimd.memset(bl[:], 0.0).then_inc(b_set, 1)

                    def step(t, p):
                        if not is_t(t, 0):
                            pool.wait_ge(at_copied, t)
                            hold(pool)
                            nc.gpsimd.affine_select(
                                out=a_t[:], in_=a_t[:], compare_op=ALU.is_ge, fill=0.0, base=0,
                                pattern=[[0, 2], [0, 2], [1, P]], channel_multiplier=-1).then_inc(at_masked, 1)
                        if not (isinstance(t, int) and t < 2):
                            scale_y(t, p)
                        if not (isinstance(t, int) and t >= T - 1):
                            rstd_x(pool, t + (T + 1), 1 - p)
                        if not is_t(t, 0):
                            pool.wait_ge(ss4_ready, 4 * t)
                            hold(pool)
                            nc.gpsimd.tensor_scalar(ms4[:], ss4[:], 1.0 / GV, EPS, ALU.mult, ALU.add)\
                                .then_inc(ms4_ready, 1)
                            pool.wait_ge(ms4_ready, t)
                            nc.gpsimd.tensor_tensor(rs4[:], ms4[:], half[:, 0:GH], ALU.pow)\
                                .then_inc(rs4_ready, 1)
                            pool.wait_ge(rs4_ready, t)
                            pool.wait_ge(mix_loaded, 16 * t)
                            g = mix[:, AW:D].rearrange("p (h v) -> p h v", v=GV)
                            nc.gpsimd.tensor_tensor(g, g, rs4[:, :].unsqueeze(2).to_broadcast((P, GH, GV)),
                                                    ALU.mult).then_inc(mixg_scaled, 1)

                    def scale_y(t, p):
                        pool.wait_ge(ssy_ready, t - 1)
                        hold(pool)
                        nc.gpsimd.tensor_scalar(msy[:, p:p + 1], ssy[:, p:p + 1], 1.0 / D, EPS,
                                                ALU.mult, ALU.add).then_inc(msy_ready, 1)
                        pool.wait_ge(msy_ready, t - 1)
                        nc.gpsimd.tensor_tensor(rsy[:, p:p + 1], msy[:, p:p + 1], half[:, 0:1], ALU.pow)\
                            .then_inc(rsy_ready, 1)

                    steps(pool, step)
                    scale_y(T + 1, 1)

                @block.scalar
                def _(act):
                    act.wait_ge(acc_filled, 4 * T)
                    for k in range(2 * KT):
                        act.wait_ge(raw_loaded[k % 2], 32 * HALF + 16 * (k // 2 + 1))
                        if k < KT:
                            if k == 0:
                                act.wait_ge(raw_r_loaded, 16)
                            nc.scalar.activation(w_r[:, k, 0:GR], stage_r[:, k, :], ACT.Copy,
                                                 scale=gain_col[:, k:k + 1])
                            nc.scalar.activation(wb[:, 0, k, :], stage[:, k % 2, :], ACT.Copy,
                                                 scale=gain_col[:, k:k + 1]).then_inc(w_hi, 1)
                        elif k < KT + HALF:
                            nc.scalar.activation(wo[:, 0, k - KT, :], stage[:, k % 2, :], ACT.Copy)\
                                .then_inc(w_hi, 1)
                        else:
                            nc.scalar.activation(wo[:, 0, k - KT, :], stage[:, k % 2, :], ACT.Copy,
                                                 scale=gla_gain_col[:, 0:1]).then_inc(w_hi, 1)
                    pass_a_done(act)

                    def hi_part(t, k, dst, counter):
                        act.wait_ge(b_tp_filled, b_filled(t, k))
                        nc.scalar.activation(dst, tp[k % 2][:, :].rearrange("p (k c) -> p k c", c=P),
                                             ACT.Copy).then_inc(counter, 1)

                    def square_y(t, p):
                        act.wait_ge(b_acc_drained[1], acc_prior(t - 1, 3) + 1)
                        nc.scalar.activation(junk_y[:], yb[:, p, :], ACT.Square,
                                             accum_out=ssy[:, p:p + 1]).then_inc(ssy_ready, 1)

                    def step(t, p):
                        first, tail = is_t(t, 0), is_t(t, T)
                        if not (isinstance(t, int) and t < 2):
                            square_y(t, p)
                        if not (isinstance(t, int) and t >= T - 1):
                            square_x(act, t + (T + 1), 1 - p, 8 * t + 8 * T + (16 if p == 0 else 24))
                        if not tail:
                            act.wait_ge(r_filled, 2 * t + 1)
                            nc.scalar.activation(r_t[0:2 * GR, :], rb[0:2 * GR, 0:P], ACT.Copy)\
                                .then_inc(rt_copied, 1)
                        if not first:
                            act.wait_ge(at_filled, t)
                            nc.scalar.activation(a_t[:, 0, :, :], at[0][:, 0:2 * P].rearrange(
                                "p (j c) -> p j c", c=P), ACT.Copy)
                            nc.scalar.activation(a_t[:, 1, :, :], at[1][:, 0:2 * P].rearrange(
                                "p (j c) -> p j c", c=P), ACT.Copy).then_inc(at_copied, 1)
                        if not tail:
                            act.wait_ge(b_acc_filled, acc_use(t, 0) + 1)
                            nc.scalar.activation(qk[:, 0:GKW], acc[0][:, 0:GKW], ACT.Copy,
                                                 scale=GK ** -0.5)
                            nc.scalar.activation(qk[:, GKW:], acc[0][:, GKW:], ACT.Copy)\
                                .then_inc(b_acc_drained[0], 1)
                            act.wait_ge(r_filled, 2 * t + 2)
                            if not first:
                                act.wait_ge(ls_ready, t)
                            y = rb[:, 256:512]
                            nc.scalar.activation(l_b[:], y, ACT.Abs).then_inc(l_ready, 1)
                            act.wait_ge(l_ready, 3 * t + 1)
                            nc.scalar.activation(l_b[:], l_b[:], ACT.Exp, scale=-1.0).then_inc(l_ready, 1)
                            act.wait_ge(l_ready, 3 * t + 2)
                            nc.scalar.activation(l_b[:], l_b[:], ACT.Ln, bias=1.0).then_inc(l_ready, 1)
                        if not first:
                            hi_part(t, 0, mix_t[:, 0, 0:HALF, :], mix_hi)
                        if not tail:
                            act.wait_ge(fsum_ready, t + 1)
                            nc.scalar.activation(fexp[:], fsum[:], ACT.Exp, scale=1.0 / GATE_NORM)\
                                .then_inc(fexp_ready, 1)
                        if not first:
                            act.wait_ge(o_filled, t)
                            if not is_t(t, 1):
                                act.wait_ge(ms4_ready, t - 1)
                            for h in range(GH):
                                nc.scalar.activation(junk_g[:, h, :], o_b[h % 2][:, h // 2, :], ACT.Square,
                                                     accum_out=ss4[:, h:h + 1]).then_inc(ss4_ready, 1)
                        if not tail:
                            act.wait_ge(b_mid, t + 1)
                            bb = b_b[:, :, :, :].rearrange("p j c i -> p j (c i)")
                            nc.scalar.activation(e_up[:], bb, ACT.Exp, scale=1.0 / GATE_NORM)
                            nc.scalar.activation(e_dn[:], bb, ACT.Exp, scale=-1.0 / GATE_NORM)\
                                .then_inc(decay_ready, 1)
                            act.wait_ge(b_acc_filled, acc_use(t, 1) + 1)
                            nc.scalar.activation(vb[:], acc[1][:, :], ACT.Copy).then_inc(b_acc_drained[1], 1)
                        if not first:
                            hi_part(t, 1, mix_t[:, 0, HALF:KT, :], mix_hi)
                        if not (isinstance(t, int) and t >= T - 1):
                            for k in range(2):
                                hi_part(t, 3 + k, ht[:, 1 - p, 0, HALF * k:HALF * k + HALF, :], h_hi)
                        if not tail:
                            act.wait_ge(b_tp_filled, b_filled(t, 5))
                            nc.scalar.activation(k_tok[:], tp[1][:, 0:2 * P].rearrange(
                                "p (j c) -> p j c", c=P), ACT.Copy).then_inc(b_tp_drained[1], 1)

                    steps(act, step)
                    square_y(T + 1, 1)

                @block.vector
                def _(dve):
                    for k in range(2 * KT):
                        dve.wait_ge(w_hi, KT + k + 1)
                        if k < KT:
                            nc.vector.scalar_tensor_tensor(
                                out=w_r[:, k, GR:], in0=stage_r[:, k, :], scalar=gain_col[:, k:k + 1],
                                in1=w_r[:, k, 0:GR].bitcast(F32), op0=ALU.mult, op1=ALU.subtract)
                            nc.vector.scalar_tensor_tensor(
                                out=wb[:, 1, k, :], in0=stage[:, k % 2, :], scalar=gain_col[:, k:k + 1],
                                in1=wb[:, 0, k, :].bitcast(F32), op0=ALU.mult, op1=ALU.subtract)\
                                .then_inc(w_lo, 1)
                        elif k < KT + HALF:
                            nc.vector.tensor_tensor(wo[:, 1, k - KT, :], stage[:, k % 2, :],
                                                    wo[:, 0, k - KT, :].bitcast(F32), ALU.subtract)\
                                .then_inc(w_lo, 1)
                        else:
                            nc.vector.scalar_tensor_tensor(
                                out=wo[:, 1, k - KT, :], in0=stage[:, k % 2, :], scalar=gla_gain_col[:, 0:1],
                                in1=wo[:, 0, k - KT, :].bitcast(F32), op0=ALU.mult, op1=ALU.subtract)\
                                .then_inc(w_lo, 1)
                    dve.wait_ge(b_set, 2)
                    dve.wait_ge(gain_loaded_b, 16)

                    def lo_part(t, k, dst, hi, counter, count):
                        dve.wait_ge(counter, count)
                        nc.vector.tensor_tensor(dst, tp[k % 2][:, :].rearrange("p (k c) -> p k c", c=P),
                                                hi.bitcast(F32), ALU.subtract).then_inc(b_tp_drained[k % 2], 1)

                    def finish(t, p):
                        dve.wait_ge(rsy_ready, t - 1)
                        nc.vector.scalar_tensor_tensor(out=yb[:, p, :], in0=yb[:, p, :], scalar=rsy[:, p:p + 1],
                                                       in1=gain_row[:], op0=ALU.mult, op1=ALU.mult)\
                            .then_inc(y_scaled, 1)

                    def step(t, p):
                        first, tail = is_t(t, 0), is_t(t, T)
                        if not (isinstance(t, int) and t >= T - 1):
                            scale_x(dve, t + (T + 1), 1 - p)
                        if not (isinstance(t, int) and t < 2):
                            finish(t, p)
                        if not (first or tail):
                            dve.wait_ge(u_filled, t)
                            dve.wait_ge(state_ready, 2 * t)
                            nc.vector.tensor_tensor(state_x[:], u_b, state[:], ALU.add).then_inc(x_state, 1)
                        if not tail:
                            dve.wait_ge(l_ready, 3 * t + 3)
                            nc.vector.scalar_tensor_tensor(out=ls_b[:], in0=rb[:, 256:512], scalar=0.0,
                                                           in1=l_b[:], op0=ALU.min, op1=ALU.subtract)\
                                .then_inc(ls_ready, 1)
                            dve.wait_ge(ls_ready, t + 1)
                            if not first:
                                dve.wait_ge(decay_ready, t)
                            nc.vector.tensor_tensor_scan(
                                b_b[:].rearrange("p j c i -> p (j c i)"), scan_mask[:], ls_b[:], 0.0,
                                ALU.mult, ALU.add).then_inc(b_scanned, 1)
                            dve.wait_ge(b_scanned, t + 1)
                            nc.vector.tensor_copy(bl[:, p, :, :], b_b[:, :, :, GC - 1]).then_inc(bl_ready, 1)
                            dve.wait_ge(bl_ready, t + 1)
                            nc.vector.tensor_tensor(fsum[:], bl[:, p, :, 0], bl[:, 1 - p, :, 1], ALU.add)\
                                .then_inc(fsum_ready, 1)
                            nc.vector.tensor_tensor(b_b[:, :, 0, :], b_b[:, :, 0, :],
                                                    bl[:, p, :, 0:1].to_broadcast((P, 2, GC)),
                                                    ALU.subtract).then_inc(b_mid, 1)
                        if not first:
                            lo_part(t, 0, mix_t[:, 1, 0:HALF, :], mix_t[:, 0, 0:HALF, :], mix_hi, 2 * t - 1)
                            dve.wait_ge(o_filled, t)
                        if not tail:
                            dve.wait_ge(fexp_ready, t + 1)
                            if not first:
                                dve.wait_ge(x_state, t)
                            for j in range(2):
                                nc.vector.tensor_scalar(state[:, j, :], state_x[:, j, :], fexp[:, j:j + 1], None,
                                                        ALU.mult).then_inc(state_ready, 1)
                        if not first:
                            dve.wait_ge(mixg_scaled, t)
                            for o in range(2):
                                last = nc.vector.tensor_tensor(mix_g[:, o], o_b[o], mix_g[:, o], ALU.mult)
                            last.then_inc(mix_ready, 1)
                            lo_part(t, 1, mix_t[:, 1, HALF:KT, :], mix_t[:, 0, HALF:KT, :], mix_hi, 2 * t)
                        if not tail:
                            dve.wait_ge(decay_ready, t + 1)
                            dve.wait_ge(b_tp_filled, b_filled(t, 2))
                            nc.vector.tensor_tensor(q_dec[:], tp[0][:, 0:2 * P].rearrange(
                                "p (j c) -> p j c", c=P), e_up[:], ALU.mult)
                            nc.vector.tensor_tensor(k_dec[:], tp[0][:, 2 * P:4 * P].rearrange(
                                "p (j c) -> p j c", c=P), e_dn[:], ALU.mult).then_inc(b_tp_drained[0], 1)
                        if not (isinstance(t, int) and t >= T - 1):
                            for k in range(2):
                                lo_part(t, 3 + k, ht[:, 1 - p, 1, HALF * k:HALF * k + HALF, :],
                                        ht[:, 1 - p, 0, HALF * k:HALF * k + HALF, :], h_hi,
                                        2 * t + (2 * T + 3 + k))
                        if not first:
                            for g in range(2):
                                dve.wait_ge(b_acc_filled, acc_use(t, 2 + g) + 1)
                                if g == 0:
                                    dve.wait_ge(y_loaded[1 - p], 8 * t + (8 if p else 0))
                                half_y = yb[:, 1 - p, 512 * g:512 * g + 512]
                                nc.vector.tensor_tensor(half_y, acc[g][:, :], half_y, ALU.add)\
                                    .then_inc(b_acc_drained[g], 1)

                    steps(dve, step)
                    finish(T + 1, 1)

                @block.tensor
                def _(pe):
                    def step(t, p):
                        first, second, tail = is_t(t, 0), is_t(t, 1), is_t(t, T)
                        last_prep = isinstance(t, int) and t >= T - 1

                        def products(dst, xs, slot_kts, w, cols, start_kt, stop_kt):
                            for kt in slot_kts:
                                hi, lo = xs(0, kt), xs(1, kt)
                                if first and w is wb:
                                    pe.wait_ge(w_lo, KT + kt + 1)
                                if second and w is wo:
                                    pe.wait_ge(w_lo, 2 * KT + kt + 1)
                                for i, (a, s) in enumerate(((hi, 0), (hi, 1), (lo, 0))):
                                    last = nc.tensor.matmul(dst, a, w[:, s, kt, cols],
                                                            start=(kt == start_kt and i == 0),
                                                            stop=(kt == stop_kt and i == 2))
                            return last

                        def hx(s, kt):
                            return ht[:, p, s, kt, :]

                        def mx_(s, kt):
                            return mix_t[:, s, kt, :]

                        def acc_free(g):
                            if not (first or (second and acc_prior(t, g) < 1)):
                                pe.wait_ge(b_acc_drained[g % 2], acc_prior(t, g))

                        def output(g, kts):
                            if 0 in kts:
                                acc_free(2 + g)
                            last = products(acc[g][:, :], mx_, kts, wo, slice(512 * g, 512 * g + 512), 0, KT - 1)
                            if KT - 1 in kts:
                                last.then_inc(b_acc_filled, 1)

                        def tp_free(k):
                            if not (first and k < 4):
                                pe.wait_ge(b_tp_drained[k % 2], b_prior(t, k))

                        if first:
                            pe.wait_ge(mixa_ready, T)
                            for b in range(3):
                                pe.wait_ge(tp_drained[b], 3 * T + (1, 1, 0)[b])
                        if not tail:
                            if not first:
                                for k in range(2):
                                    b_data(pe, t - 1, 3 + k)
                            if not first:
                                pe.wait_ge(ls_ready, t)
                            for kt in range(KT):
                                if first:
                                    pe.wait_ge(w_lo, KT + kt + 1)
                                for s in range(2):
                                    last = nc.tensor.matmul(rb[0:2 * GR, 0:P], w_r[:, kt, :], hx(s, kt),
                                                            start=(kt == 0 and s == 0),
                                                            stop=(kt == KT - 1 and s == 1))
                            last.then_inc(r_filled, 1)
                        if not first:
                            b_data(pe, t - 1, 2)
                            if not second:
                                pe.wait_ge(x_state, t - 1)
                                pe.wait_ge(at_copied, t - 1)
                                pe.wait_ge(mix_ready, t - 1)
                            for o in range(2):
                                rows = slice(GK * o, GK * o + GK)
                                for j in range(2):
                                    last = nc.tensor.matmul(at[o][:, j * P:(j + 1) * P], k_dec[rows, j, :],
                                                            q_dec[rows, j, :], start=True, stop=True)
                            last.then_inc(at_filled, 1)
                        if not tail:
                            acc_free(0)
                            products(acc[0][:, :], hx, range(HALF), wb, slice(B_QK, B_V), 0, KT - 1)
                        if not (first or tail):
                            b_data(pe, t - 1, 5)
                            acc_data(pe, t - 1, 1)
                            pe.wait_ge(at_copied, t)
                            for h in range(GH):
                                rows = slice(GK * (h % 2), GK * (h % 2) + GK)
                                last = nc.tensor.matmul(u_b[rows, h // 2, :], k_tok[:, h // 2, rows],
                                                        vb[:, h * GV:(h + 1) * GV], start=True, stop=True)
                            last.then_inc(u_filled, 1)
                        if tail:
                            acc_data(pe, t - 1, 1)
                        if not tail:
                            products(acc[0][:, :], hx, range(HALF, KT), wb, slice(B_QK, B_V), 0, KT - 1)\
                                .then_inc(b_acc_filled, 1)
                            pe.wait_ge(rt_copied, t + 1)
                            for j in range(2):
                                last = nc.tensor.matmul(rb[:, 256 + j * P:256 + (j + 1) * P],
                                                        w_up[:, j * P:(j + 1) * P], r_t[:],
                                                        start=True, stop=True)
                            last.then_inc(r_filled, 1)
                        if not first:
                            pe.wait_ge(at_masked, t)
                            pe.wait_ge(state_ready, 2 * t)
                            for h in range(GH):
                                rows = slice(GK * (h % 2), GK * (h % 2) + GK)
                                dst = o_b[h % 2][:, h // 2, :]
                                nc.tensor.matmul(dst, q_dec[rows, h // 2, :], state[rows, h // 2, :],
                                                 start=True, stop=False)
                                last = nc.tensor.matmul(dst, a_t[:, h % 2, h // 2, :],
                                                        vb[:, h * GV:(h + 1) * GV], start=False, stop=True)
                            last.then_inc(o_filled, 1)
                            tp_free(0)
                            pe.wait_ge(mix_loaded, 16 * t)
                            for c in range(HALF):
                                last = nc.tensor.transpose(tp[0][:, c * P:(c + 1) * P],
                                                           mix[:, c * P:(c + 1) * P], ident[:])
                            last.then_inc(b_tp_filled, 1)
                        if not tail:
                            acc_free(1)
                            products(acc[1][:, :], hx, range(KT), wb, slice(B_V, NB), 0, KT - 1)\
                                .then_inc(b_acc_filled, 1)
                        if not first:
                            tp_free(1)
                            pe.wait_ge(mix_ready, t)
                            for c in range(HALF):
                                last = nc.tensor.transpose(tp[1][:, c * P:(c + 1) * P],
                                                           mix[:, AW + c * P:AW + (c + 1) * P], ident[:])
                            last.then_inc(b_tp_filled, 1)
                        if not tail:
                            tp_free(2)
                            acc_data(pe, t, 0)
                            for c in range(4):
                                last = nc.tensor.transpose(tp[0][:, c * P:(c + 1) * P],
                                                           qk[:, c * P:(c + 1) * P], ident[:])
                            last.then_inc(b_tp_filled, 1)
                        if not first:
                            if tail:
                                pe.wait_ge(b_tp_drained[0], b_prior(t, 0) + 1)
                            else:
                                b_data(pe, t, 0)
                            output(0, range(HALF))
                        if not last_prep:
                            pe.wait_ge(h_ready, t + (T + 2))
                            for k in range(2):
                                tp_free(3 + k)
                                for c in range(HALF):
                                    kt = HALF * k + c
                                    last = nc.tensor.transpose(tp[(3 + k) % 2][:, c * P:(c + 1) * P],
                                                               xb[:, 1 - p, kt * P:(kt + 1) * P], ident[:])
                                last.then_inc(b_tp_filled, 1)
                        if not first:
                            b_data(pe, t, 1)
                            output(0, range(HALF, KT))
                        if not tail:
                            if last_prep:
                                b_data(pe, t, 1)
                            else:
                                tp_free(5)
                            b_data(pe, t, 2)
                            for j in range(2):
                                last = nc.tensor.transpose(tp[1][:, j * P:(j + 1) * P], k_dec[:, j, :], ident[:])
                            last.then_inc(b_tp_filled, 1)
                        if not first:
                            output(1, range(KT))

                    steps(pe, step)


_INS = ["x", "norm_gain", "w_in", "w_gate_up", "b_gate", "rel_bias", "sinks", "gla_norm_gain", "w_out",
        "final_norm_gain"]


def kernel(**inputs):
    import numpy as _np
    import concourse.bacc as _bacc
    from concourse import mybir as _mybir
    from concourse.bass_utils import run_bass_kernel_spmd as _run

    nc = _bacc.Bacc("TRN2", target_bir_lowering=False, num_devices=1, dynamic_dma_scratch_size=1024)
    arrays, args = {}, []
    for name in _INS:
        a = _np.ascontiguousarray(inputs[name])
        arrays[f"in_{name}_dram"] = a
        args.append(nc.dram_tensor(f"in_{name}_dram", a.shape, _mybir.dt.from_np(a.dtype),
                                   kind="ExternalInput").ap())
    args.append(nc.dram_tensor("out_0_dram", (1, S, D), F32, kind="ExternalOutput").ap())
    hybrid_block(nc, *args)
    r = _run(nc, [arrays], core_ids=[0])
    return r.results[0]["out_0_dram"]
```

```python
from contextlib import ExitStack

import numpy as np

import concourse.bass as bass
from concourse import mybir

F32 = mybir.dt.float32
F32R = mybir.dt.float32r
BF16 = mybir.dt.bfloat16
ALU = mybir.AluOpType
ACT = mybir.ActivationFunctionType

P = 128
D = 1024
S = 2048
T = S // P
KT = D // P
EPS = 1e-6
NEG = -1e30

AH, AKV, AD = 8, 2, 64
AG = AH // AKV
AW, AKW = AH * AD, AKV * AD
NUM_BUCKETS, MAX_DISTANCE, WINDOW = 32, 128, 128
GH, GK, GV, GR, GC = 4, 64, 128, 16, 64
GKW, GW = GH * GK, GH * GV
GATE_NORM = 16.0

C_Q, C_KV = 0, AW
C_ZA = C_KV + 2 * AKW
C_QK = C_ZA + AW
C_V = C_QK + 2 * GKW
C_ZG = C_V + GW
C_R = C_ZG + GW
N_IN = C_R + GR

HALF = KT // 2
NW = 512

G_ZA, G_ZG, G_KV, G_Q, G_QK, G_V, G_OUT0, G_OUT1 = range(8)
G_COLS = ((C_ZA, AW), (C_ZG, GW), (C_KV, 2 * AKW), (C_Q, AW), (C_QK, 2 * GKW), (C_V, GW), (0, NW), (NW, NW))


def split_count(g, kt):
    return KT * g + kt + 1


def bucket(n):
    exact = NUM_BUCKETS // 2
    if n < exact:
        return n
    large = exact + int(np.log(n / exact) / np.log(MAX_DISTANCE / exact) * (NUM_BUCKETS - exact))
    return min(large, NUM_BUCKETS - 1)


def bucket_runs():
    runs = []
    for j in range(P, 2 * P):
        b = bucket(2 * P - 1 - j)
        if runs and runs[-1][2] == b:
            runs[-1][1] = j + 1
        else:
            runs.append([j, j + 1, b])
    return runs


def a_filled(t, k):
    return 9 * t + (k - 3)


def a_bank(k):
    return (k + 2) % 3


def a_prior(t, k):
    return 3 * t + (k - 4) // 3


def b_filled(t, k):
    return 4 * t + (k - 1)


def b_prior(t, k):
    return 2 * t + (k // 2 - 1)


def acc_use(t, g):
    if isinstance(t, int) and t == 0:
        return g
    if isinstance(t, int) and t == T:
        return 4 * t - 4 + g
    return 4 * t + (g - 2)


def acc_prior(t, g):
    if isinstance(t, int) and t == 0:
        return 0
    if isinstance(t, int) and t == T:
        return 2 * t + (g - 4) // 2
    return 2 * t + (g // 2 - 1)


def is_t(t, n):
    return isinstance(t, int) and t == n


def steps(eng, body):
    body(0, 0)
    body(1, 1)
    with eng.Fori(2, T - 2, 2) as t:
        body(t, 0)
        body(t + 1, 1)
    for t in range(T - 2, T + 1):
        body(t, t % 2)


def hybrid_block(nc, x, norm_gain, w_in, w_gate_up, b_gate, rel_bias, sinks, gla_norm_gain, w_out,
                 final_norm_gain, out):
    x_t = x.rearrange("o (t p) d -> (o t) p d", p=P)
    out_t = out.rearrange("o (t p) d -> (o t) p d", p=P)
    w_in_k = w_in.rearrange("l (k p) n -> (l p) k n", p=P)
    w_out_k = w_out.rearrange("l (k p) n -> (l p) k n", p=P)
    mix_dram = nc.dram_tensor("mix_scratch", (T, P, D), F32).ap()
    ht_dram = nc.dram_tensor("ht_scratch", (T, P, 2 * KT * P), F32).ap()
    line_dram = nc.dram_tensor("bias_lines", (AH, P, 3 * P), F32)

    with ExitStack() as ctx:
        def sb(name, shape, dt=F32):
            return ctx.enter_context(nc.sbuf_tensor(name, shape, dt))

        def bank(name):
            return ctx.enter_context(nc.psum_tensor(name, [P, 512], F32))

        def sem(name):
            return ctx.enter_context(nc.semaphore(name))

        w_block = [sb(f"w_block{i}", [P, 2, KT, NW], F32R) for i in range(3)]
        xb = sb("xb", [P, 2, D])
        ht = sb("ht", [P, 2, 2, KT, P], F32R)
        junk = sb("junk", [P, D], BF16)
        ez = sb("ez", [P, 4, AW])
        raw_out = ez[:, :, :].rearrange("p (i m) (c n) -> p i (m c) n", i=2, n=2 * AKW)
        stage_r = sb("stage_r", [P, KT, GR])
        ident = sb("ident", [P, P])
        gain_col = sb("gain_col", [P, KT])
        gla_gain_col = sb("gla_gain_col", [P, 1])
        half = sb("half", [P, AH])
        ss = sb("ss", [P, 2])
        ms = sb("ms", [P, 2])
        rstd = sb("rstd", [P, 2])
        w_r = sb("w_r", [P, KT, 2 * GR], F32R)
        r_t = sb("r_t", [2 * GR + 1, P])
        w_up = sb("w_up", [2 * GR + 1, GKW])
        scan_mask = sb("scan_mask", [P, 2 * P])
        sink = sb("sink", [P, AH])
        mx = sb("mx", [P, AH])
        nmx = sb("nmx", [P, AH])
        sinkd = sb("sinkd", [P, AH])
        esink = sb("esink", [P, AH])
        psum_row = sb("psum_row", [P, AH])
        den = sb("den", [P, AH])
        rden = sb("rden", [P, AH])
        rel_t = sb("rel_t", [AH, NUM_BUCKETS])

        x_loaded = [sem(f"x_loaded{i}") for i in range(2)]
        const_loaded = sem("const_loaded")
        gain_loaded = sem("gain_loaded")
        const_set = sem("const_set")
        held = sem("held")
        ident_set = sem("ident_set")
        line_set = sem("line_set")
        line_stored = sem("line_stored")
        bias_loaded = sem("bias_loaded")
        bias_widened = sem("bias_widened")
        raw_loaded = [sem(f"raw_loaded{i}") for i in range(HALF)]
        raw_out_loaded = [sem(f"raw_out_loaded{i}") for i in range(2)]
        raw_r_loaded = sem("raw_r_loaded")
        w_hi = sem("w_hi")
        w_lo = sem("w_lo")
        w_r_hi = sem("w_r_hi")
        w_r_lo = sem("w_r_lo")
        ss_ready = sem("ss_ready")
        ms_ready = sem("ms_ready")
        rstd_ready = sem("rstd_ready")
        h_ready = sem("h_ready")
        h_hi = sem("h_hi")
        ht_stored = [sem(f"ht_stored{i}") for i in range(2)]
        ht_loaded = [sem(f"ht_loaded{i}") for i in range(2)]

        def settle(eng):
            eng.wait_ge(ident_set, 2)

        def hold(eng):
            eng.sem_inc(held, 1)

        def square_x(act, n, slot, loads):
            act.wait_ge(x_loaded[slot], loads)
            nc.scalar.activation(junk[:], xb[:, slot, :], ACT.Square,
                                 accum_out=ss[:, slot:slot + 1]).then_inc(ss_ready, 1)

        def rstd_x(pool, n, slot):
            pool.wait_ge(ss_ready, n + 1)
            hold(pool)
            nc.gpsimd.tensor_scalar(ms[:, slot:slot + 1], ss[:, slot:slot + 1], 1.0 / D, EPS,
                                    ALU.mult, ALU.add).then_inc(ms_ready, 1)
            pool.wait_ge(ms_ready, n + 1)
            nc.gpsimd.tensor_tensor(rstd[:, slot:slot + 1], ms[:, slot:slot + 1], half[:, 0:1],
                                    ALU.pow).then_inc(rstd_ready, 1)

        def scale_x(dve, n, slot):
            dve.wait_ge(rstd_ready, n + 1)
            nc.vector.tensor_scalar(xb[:, slot, :], xb[:, slot, :], rstd[:, slot:slot + 1], None,
                                    ALU.mult).then_inc(h_ready, 1)

        def raw_pair(g, i):
            if g == G_OUT1:
                return raw_out[:, i % 2]
            return raw_w[:, i]

        def load_raw(sp, g, i):
            c0, n = G_COLS[g]
            if g == G_OUT1:
                if i >= 2:
                    sp.wait_ge(w_lo, split_count(g, 2 * i - 3))
                else:
                    sp.wait_ge(gate_ready, 2 * T)
                loaded = raw_out_loaded[i % 2]
            else:
                if g > 0:
                    sp.wait_ge(w_lo, split_count(g - 1, 2 * i + 1))
                loaded = raw_loaded[i]
            src = w_out_k if g >= G_OUT0 else w_in_k
            pieces = n // (2 * AKW)
            for r in range(2):
                sp.dma_start(raw_pair(g, i)[:, pieces * r:pieces * r + pieces, :],
                             src[:, 2 * i + r, c0:c0 + n].rearrange("p (c n) -> p c n", n=2 * AKW))\
                  .then_inc(loaded, 16)

        def split_views(g, kt):
            pieces = G_COLS[g][1] // (2 * AKW)
            raw = raw_pair(g, kt // 2)[:, pieces * (kt % 2):pieces * (kt % 2) + pieces, :]
            dst = w_home[g][:, :, kt, :].rearrange("p s (c n) -> p s c n", n=2 * AKW)
            if g < G_OUT0:
                gain = gain_col[:, kt:kt + 1]
            else:
                gain = gla_gain_col[:, 0:1] if kt >= HALF else 1.0
            return raw, dst, gain

        def split_hi(act, g, kts):
            for kt in kts:
                raw, dst, gain = split_views(g, kt)
                if g >= G_QK and kt == 0:
                    act.wait_ge(acc_filled, 4 * T - (3, 2, 0, 0)[g - G_QK])
                if g == G_OUT1 and kt == 0:
                    act.wait_ge(w_lo, split_count(G_OUT0, KT - 1))
                if g == G_OUT1:
                    act.wait_ge(raw_out_loaded[(kt // 2) % 2], 32 * (kt // 4 + 1))
                else:
                    act.wait_ge(raw_loaded[kt // 2], 32 * (g + 1))
                nc.scalar.activation(dst[:, 0], raw, ACT.Copy, scale=gain).then_inc(w_hi, 1)

        def split_lo(dve, g, kts):
            for kt in kts:
                raw, dst, gain = split_views(g, kt)
                dve.wait_ge(w_hi, split_count(g, kt))
                nc.vector.scalar_tensor_tensor(out=dst[:, 1], in0=raw, scalar=gain, in1=dst[:, 0].bitcast(F32),
                                               op0=ALU.mult, op1=ALU.subtract).then_inc(w_lo, 1)

        def split_r_hi():
            nc.scalar.wait_ge(raw_r_loaded, 16)
            for kt in range(KT):
                nc.scalar.activation(w_r[:, kt, 0:GR], stage_r[:, kt, :], ACT.Copy,
                                     scale=gain_col[:, kt:kt + 1]).then_inc(w_r_hi, 1)

        def split_r_lo():
            for kt in range(KT):
                nc.vector.wait_ge(w_r_hi, kt + 1)
                nc.vector.scalar_tensor_tensor(
                    out=w_r[:, kt, GR:], in0=stage_r[:, kt, :], scalar=gain_col[:, kt:kt + 1],
                    in1=w_r[:, kt, 0:GR].bitcast(F32), op0=ALU.mult, op1=ALU.subtract).then_inc(w_r_lo, 1)

        def ht_bytes(slot):
            return ht[:, slot].rearrange("p s k c -> p (s k c)").bitcast(F32)

        acc = [bank(f"acc{i}") for i in range(2)]
        tp = [bank(f"tp{i}") for i in range(3)]
        sc = [bank(f"sc{i}") for i in range(2)]
        oa = bank("oa")

        with ExitStack() as pa:
            def sba(name, shape, dt=F32):
                return pa.enter_context(nc.sbuf_tensor(name, shape, dt))

            w_kv = sba("w_kv", [P, 2, KT, 2 * AKW], F32R)
            raw_w = sba("raw_w", [P, HALF, 4, 2 * AKW])
            probs = sba("probs", [P, AH, 2 * P])
            probs_t = sba("probs_t", [P, AH, 2, P])
            bias = sba("bias", [P, AH, 3 * P])
            q_s = sba("q_s", [P, AW])
            q2t = sba("q2t", [P, AH, P], F32R)
            k_s = sba("k_s", [P, AKV, 2, AD])
            k2t = sba("k2t", [P, 2, 2, AKV, P], F32R)
            va = sba("va", [P, 2, AKV, AD])
            gate_a = sba("gate_a", [P, 2, AW])
            gate_g = sba("gate_g", [P, 2, GW])
            mixa = sba("mixa", [P, 2, AW])
            line = mixa[0:AH, 0, 0:3 * P]
            zline = mixa[0:AH, 1, 0:P]
            acc_filled = sem("acc_filled")
            acc_drained = [sem(f"acc_drained{i}") for i in range(2)]
            tp_filled = sem("tp_filled")
            tp_drained = [sem(f"tp_drained{i}") for i in range(3)]
            sc_filled = sem("sc_filled")
            sc_drained = [sem(f"sc_drained{i}") for i in range(2)]
            oa_filled = sem("oa_filled")
            q_hi = sem("q_hi")
            k_hi = sem("k_hi")
            nmx_ready = sem("nmx_ready")
            sinkd_ready = sem("sinkd_ready")
            exp_ready = sem("exp_ready")
            esink_ready = sem("esink_ready")
            den_ready = sem("den_ready")
            rden_ready = sem("rden_ready")
            e_ready = sem("e_ready")
            e1_ready = sem("e1_ready")
            rec_ready = sem("rec_ready")
            gate_ready = sem("gate_ready")
            gate_scaled = sem("gate_scaled")
            mixa_ready = sem("mixa_ready")
            mixa_stored = sem("mixa_stored")
            gate_stored = sem("gate_stored")

            runs = bucket_runs()

            def q_views(k, odd):
                rows = slice(AD * odd, AD * odd + AD)
                return (rows, slice(4 * k + odd, 4 * k + 4, 2),
                        tp[a_bank(k)][rows, 0:2 * P].rearrange("p (c i) -> p c i", i=P))

            def a_data(eng, t, k):
                eng.wait_ge(tp_drained[a_bank(k)], a_prior(t, k) + 1)

        with ExitStack() as pb:
            def sbb(name, shape, dt=F32):
                return pb.enter_context(nc.sbuf_tensor(name, shape, dt))

            w_out1 = sbb("w_out1", [P, 2, KT, NW], F32R)
            yb = sbb("yb", [P, 2, D])
            mix = sbb("mix", [P, D])
            mix_t = sbb("mix_t", [P, 2, KT, P], F32R)
            gain_row = sbb("gain_row", [P, D])
            qk = sbb("qk", [P, 2 * GKW])
            vb = sbb("vb", [P, GW])
            l_b = sbb("l_b", [P, 2 * P])
            ls_b = sbb("ls_b", [P, 2 * P])
            b_b = sbb("b_b", [P, 2, 2, GC])
            bl = sbb("bl", [P, 2, 2, 2])
            e_up = sbb("e_up", [P, 2, P])
            e_dn = sbb("e_dn", [P, 2, P])
            q_dec = sbb("q_dec", [P, 2, P])
            k_dec = sbb("k_dec", [P, 2, P])
            k_tok = sbb("k_tok", [P, 2, P])
            a_t = sbb("a_t", [P, 2, 2, P])
            state = sbb("state", [P, 2, GV])
            state_x = sbb("state_x", [P, 2, GV])
            junk_y = sbb("junk_y", [P, D], BF16)
            junk_g = sbb("junk_g", [P, GH, GV], BF16)
            fsum = sbb("fsum", [P, 2])
            fexp = sbb("fexp", [P, 2])
            ss4 = sbb("ss4", [P, GH])
            ms4 = sbb("ms4", [P, GH])
            rs4 = sbb("rs4", [P, GH])
            ssy = sbb("ssy", [P, 2])
            msy = sbb("msy", [P, 2])
            rsy = sbb("rsy", [P, 2])
            rb = tp[2]
            at = sc
            ob = oa
            o_b = [ob[:, 0:2 * GV].rearrange("p (j v) -> p j v", v=GV),
                   at[1][:, 256:512].rearrange("p (j v) -> p j v", v=GV)]
            mix_g = mix[:, AW:D].rearrange("p (j o v) -> p o j v", o=2, v=GV)
            u_b = at[0][:, 256:512].rearrange("p (j v) -> p j v", v=GV)

            b_acc_filled = sem("b_acc_filled")
            b_acc_drained = [sem(f"b_acc_drained{i}") for i in range(2)]
            b_tp_filled = sem("b_tp_filled")
            b_tp_drained = [sem(f"b_tp_drained{i}") for i in range(2)]
            r_filled = sem("r_filled")
            rt_copied = sem("rt_copied")
            l_ready = sem("l_ready")
            ls_ready = sem("ls_ready")
            b_scanned = sem("b_scanned")
            bl_ready = sem("bl_ready")
            b_mid = sem("b_mid")
            fsum_ready = sem("fsum_ready")
            fexp_ready = sem("fexp_ready")
            decay_ready = sem("decay_ready")
            qk_dec_ready = sem("qk_dec_ready")
            at_filled = sem("at_filled")
            at_copied = sem("at_copied")
            at_masked = sem("at_masked")
            u_filled = sem("u_filled")
            x_state = sem("x_state")
            state_ready = sem("state_ready")
            o_filled = sem("o_filled")
            ss4_ready = sem("ss4_ready")
            ms4_ready = sem("ms4_ready")
            rs4_ready = sem("rs4_ready")
            mixg_scaled = sem("mixg_scaled")
            mix_ready = sem("mix_ready")
            mix_hi = sem("mix_hi")
            mix_loaded = sem("mix_loaded")
            y_loaded = [sem(f"y_loaded{i}") for i in range(2)]
            ssy_ready = sem("ssy_ready")
            msy_ready = sem("msy_ready")
            rsy_ready = sem("rsy_ready")
            y_scaled = sem("y_scaled")
            out_stored = [sem(f"out_stored{i}") for i in range(2)]
            gain_loaded_b = sem("gain_loaded_b")
            b_set = sem("b_set")

            def pass_a_done(eng):
                eng.wait_ge(oa_filled, T)

            def b_data(eng, t, k):
                eng.wait_ge(b_tp_drained[k % 2], b_prior(t, k) + 1)

            def acc_data(eng, t, g):
                eng.wait_ge(b_acc_drained[g % 2], acc_prior(t, g) + 1)

        w_home = (w_block[0], w_block[1], w_kv, w_block[2], w_block[0], w_block[1], w_block[2], w_out1)

        with nc.Block() as block:
            @block.sync
            def _(sp):
                sp.dma_start(xb[:, 0, :], x_t[0]).then_inc(x_loaded[0], 16)
                sp.dma_start(gain_col[:], norm_gain.rearrange("l (k p) -> (l p) k", p=P),
                             allow_slow_non_contiguous=True).then_inc(gain_loaded, 16)
                for i in range(HALF):
                    load_raw(sp, G_ZA, i)
                sp.dma_start(xb[:, 1, :], x_t[1]).then_inc(x_loaded[1], 16)
                sp.dma_start(rel_t[:], rel_bias.rearrange("b h -> h b"),
                             allow_slow_non_contiguous=True).then_inc(const_loaded, 16)
                sp.dma_start(sink[:], sinks[0].partition_broadcast(P)).then_inc(const_loaded, 16)
                sp.dma_start(gla_gain_col[:], gla_norm_gain.rearrange("l v -> v l"),
                             allow_slow_non_contiguous=True).then_inc(const_loaded, 16)
                sp.dma_start(w_up[0:GR, :], w_gate_up[0]).then_inc(const_loaded, 16)
                sp.dma_start(w_up[GR:2 * GR, :], w_gate_up[0]).then_inc(const_loaded, 16)
                sp.dma_start(w_up[2 * GR:, :], b_gate).then_inc(const_loaded, 16)
                for g in (G_ZG, G_KV, G_Q):
                    for i in range(HALF):
                        load_raw(sp, g, i)
                sp.wait_ge(tp_filled, 2)
                sp.dma_start(xb[:, 0, :], x_t[2]).then_inc(x_loaded[0], 16)
                sp.wait_ge(line_set, 2 + len(runs))
                sp.dma_start(line_dram.ap(), line.unsqueeze(1).to_broadcast((AH, P, 3 * P))).then_inc(line_stored, 16)
                sp.wait_ge(line_stored, 16)
                for h in range(AH):
                    sp.dma_start(bias[:, h, 0:2 * P],
                                 bass.AP(line_dram, h * P * 3 * P + P - 1, [[3 * P - 1, P], [1, 2 * P]]))\
                      .then_inc(bias_loaded, 16)
                sp.dma_start(stage_r[:], w_in_k[:, :, C_R:N_IN]).then_inc(raw_r_loaded, 16)
                for i in range(HALF):
                    load_raw(sp, G_QK, i)

                def step(t, p, index):
                    if not is_t(t, 0):
                        settle(sp)
                        a_data(sp, t - 1, 7)
                        sp.dma_start(ht_dram[t], ht_bytes(p)).then_inc(ht_stored[p], 16)
                    settle(sp)
                    sp.wait_ge(gate_ready, 2 * t + 2)
                    sp.dma_start(mix_dram[t, :, AW:D], gate_g[:, p, :]).then_inc(gate_stored, 16)
                    if not (isinstance(t, int) and t == 0):
                        settle(sp)
                        sp.wait_ge(mixa_ready, t)
                        sp.dma_start(mix_dram[t - 1, :, 0:AW], mixa[:, 1 - p, :]).then_inc(mixa_stored, 16)
                    if not (isinstance(t, int) and t > T - 3):
                        settle(sp)
                        sp.wait_ge(tp_filled, a_filled(t, 7))
                        sp.dma_start(xb[:, 1 - p, :], x_t[index]).then_inc(x_loaded[1 - p], 16)

                step(0, 0, 3)
                step(1, 1, 4)
                with sp.Fori(2, T - 4, 2) as t:
                    step(t, 0, t + 3)
                    step(t + 1, 1, t + 4)
                for t in range(T - 4, T):
                    if t == T - 1:
                        for i in range(HALF):
                            load_raw(sp, G_V, i)
                    step(t, t % 2, (t + 3) % T)
                sp.wait_ge(ht_stored[0], 8 * T - 16)
                sp.wait_ge(ht_stored[1], 8 * T)
                sp.wait_ge(acc_filled, 4 * T)
                sp.dma_start(ht_bytes(1), ht_dram[1]).then_inc(ht_loaded[1], 16)
                for i in range(HALF):
                    load_raw(sp, G_OUT0, i)
                for i in range(2):
                    load_raw(sp, G_OUT1, i)
                sp.wait_ge(mixa_ready, T)
                sp.dma_start(mix_dram[T - 1, :, 0:AW], mixa[:, 1, :]).then_inc(mixa_stored, 16)

                sp.wait_ge(oa_filled, T)
                sp.dma_start(yb[:, 0, :], x_t[0]).then_inc(y_loaded[0], 16)
                sp.dma_start(gain_row[:], final_norm_gain.partition_broadcast(P))\
                  .then_inc(gain_loaded_b, 16)
                sp.wait_ge(mixa_stored, 16 * T)
                sp.wait_ge(gate_stored, 16 * T)
                sp.dma_start(mix[:], mix_dram[0]).then_inc(mix_loaded, 16)
                def step(t, p):
                    if not (isinstance(t, int) and t in (0, T - 1, T)):
                        settle(sp)
                        sp.wait_ge(b_acc_filled, acc_use(t - 1, 1) + 1)
                        sp.dma_start(ht_bytes(1 - p), ht_dram[t + 1]).then_inc(ht_loaded[1 - p], 16)
                    if not (isinstance(t, int) and t < 2):
                        settle(sp)
                        sp.wait_ge(y_scaled, t - 1)
                        sp.dma_start(out_t[t - 2], yb[:, p, :]).then_inc(out_stored[p], 16)
                    if is_t(t, T):
                        return
                    if not is_t(t, 0):
                        settle(sp)
                        sp.wait_ge(b_tp_filled, b_filled(t, 1))
                        sp.dma_start(mix[:], mix_dram[t]).then_inc(mix_loaded, 16)
                        if not is_t(t, 1):
                            settle(sp)
                            sp.wait_ge(out_stored[p], 8 * t if p == 0 else 8 * t - 8)
                        sp.dma_start(yb[:, p, :], x_t[t]).then_inc(y_loaded[p], 16)

                step(0, 0)
                for i in range(2, HALF):
                    load_raw(sp, G_OUT1, i)
                step(1, 1)
                with sp.Fori(2, T - 2, 2) as t:
                    step(t, 0)
                    step(t + 1, 1)
                for t in range(T - 2, T + 1):
                    step(t, t % 2)
                settle(sp)
                sp.wait_ge(y_scaled, T)
                sp.dma_start(out_t[T - 1], yb[:, (T - 1) % 2, :]).then_inc(out_stored[(T - 1) % 2], 16)
                for p in range(2):
                    sp.wait_ge(out_stored[p], 8 * T)

            @block.gpsimd
            def _(pool):
                nc.gpsimd.memset(half[:], -0.5).then_inc(const_set, 1)
                nc.gpsimd.memset(ident[:], 0.0).then_inc(ident_set, 1)
                pool.wait_ge(ident_set, 1)
                nc.gpsimd.affine_select(out=ident[:], in_=ident[:], compare_op=ALU.not_equal,
                                        fill=1.0, base=0, pattern=[[-1, P]],
                                        channel_multiplier=1).then_inc(ident_set, 1)
                nc.gpsimd.memset(r_t[:], 1.0).then_inc(const_set, 1)
                nc.gpsimd.memset(scan_mask[:], 1.0).then_inc(const_set, 1)
                pool.wait_ge(const_set, 3)
                nc.gpsimd.memset(scan_mask[:].rearrange("p (c j) -> p c j", j=GC)[:, :, 0:1], 0.0)\
                    .then_inc(const_set, 1)
                rstd_x(pool, 0, 0)
                pool.wait_ge(const_loaded, 96)
                pool.wait_ge(line_set, 2)
                for a, b, k in runs:
                    nc.gpsimd.tensor_scalar(line[:, a:b], zline[:, 0:b - a], rel_t[:, k:k + 1], None,
                                            ALU.add).then_inc(line_set, 1)

                def add_one(t, j):
                    pool.wait_ge(e_ready, 2 * t + (j + 1))
                    hold(pool)
                    nc.gpsimd.tensor_scalar(ez[:, j, :], ez[:, j, :], 1.0, None, ALU.add)\
                        .then_inc(e1_ready, 1)

                def step(t, p):
                    first = isinstance(t, int) and t == 0
                    second = is_t(t, 1)
                    tail = isinstance(t, int) and t == T
                    if not tail:
                        if not second:
                            rstd_x(pool, t + 1, 1 - p)
                        add_one(t, 0)
                        if first:
                            add_one(t, 1)
                            rstd_x(pool, 2, 0)
                        if is_t(t, 1):
                            pool.wait_ge(bias_loaded, 16 * AH)
                            nc.gpsimd.tensor_copy(bias[:, :, 2 * P:3 * P], bias[:, :, 0:P])\
                                .then_inc(bias_widened, 1)
                        pool.wait_ge(rec_ready, 4 * t + 2)
                        pool.wait_ge(acc_drained[0], 2 * t + 1)
                        if not (isinstance(t, int) and t < 2):
                            pool.wait_ge(mixa_ready, t - 1)
                        nc.gpsimd.tensor_tensor(gate_a[:, p, :], ez[:, 2, :], ez[:, 0, :], ALU.mult)\
                            .then_inc(gate_ready, 1)
                        if not first:
                            add_one(t, 1)
                    if not first:
                        pool.wait_ge(rden_ready, t)
                        if tail:
                            pool.wait_ge(gate_ready, 2 * t - 1)
                        g = gate_a[:, 1 - p, :].rearrange("p (h d) -> p h d", d=AD)
                        nc.gpsimd.tensor_tensor(g, g, rden[:, :].unsqueeze(2).to_broadcast((P, AH, AD)),
                                                ALU.mult).then_inc(gate_scaled, 1)
                    if not tail:
                        pool.wait_ge(rec_ready, 4 * t + 4)
                        pool.wait_ge(acc_drained[1], 2 * t + 1)
                        if not (isinstance(t, int) and t < 2):
                            pool.wait_ge(gate_stored, 16 * t - 16)
                        nc.gpsimd.tensor_tensor(gate_g[:, p, :], ez[:, 3, :], ez[:, 1, :], ALU.mult)\
                            .then_inc(gate_ready, 1)

                steps(pool, step)

                pass_a_done(pool)
                nc.gpsimd.memset(state_x[:], 0.0).then_inc(b_set, 1)
                nc.gpsimd.memset(bl[:], 0.0).then_inc(b_set, 1)

                def step(t, p):
                    if not is_t(t, 0):
                        pool.wait_ge(at_copied, t)
                        hold(pool)
                        nc.gpsimd.affine_select(
                            out=a_t[:], in_=a_t[:], compare_op=ALU.is_ge, fill=0.0, base=0,
                            pattern=[[0, 2], [0, 2], [1, P]], channel_multiplier=-1).then_inc(at_masked, 1)
                    if not (isinstance(t, int) and t < 2):
                        scale_y(t, p)
                    if not is_t(t, 0):
                        pool.wait_ge(ss4_ready, 4 * t)
                        hold(pool)
                        nc.gpsimd.tensor_scalar(ms4[:], ss4[:], 1.0 / GV, EPS, ALU.mult, ALU.add)\
                            .then_inc(ms4_ready, 1)
                        pool.wait_ge(ms4_ready, t)
                        nc.gpsimd.tensor_tensor(rs4[:], ms4[:], half[:, 0:GH], ALU.pow)\
                            .then_inc(rs4_ready, 1)
                        pool.wait_ge(rs4_ready, t)
                        pool.wait_ge(mix_loaded, 16 * t)
                        g = mix[:, AW:D].rearrange("p (h v) -> p h v", v=GV)
                        nc.gpsimd.tensor_tensor(g, g, rs4[:, :].unsqueeze(2).to_broadcast((P, GH, GV)),
                                                ALU.mult).then_inc(mixg_scaled, 1)

                def scale_y(t, p):
                    pool.wait_ge(ssy_ready, t - 1)
                    hold(pool)
                    nc.gpsimd.tensor_scalar(msy[:, p:p + 1], ssy[:, p:p + 1], 1.0 / D, EPS,
                                            ALU.mult, ALU.add).then_inc(msy_ready, 1)
                    pool.wait_ge(msy_ready, t - 1)
                    nc.gpsimd.tensor_tensor(rsy[:, p:p + 1], msy[:, p:p + 1], half[:, 0:1], ALU.pow)\
                        .then_inc(rsy_ready, 1)

                steps(pool, step)
                scale_y(T + 1, 1)

            @block.scalar
            def _(act):
                nc.scalar.preload_act_table_set("natural_log_exp_and_others")
                square_x(act, 0, 0, 16)
                act.wait_ge(gain_loaded, 16)

                def h_part_hi(t, k, slot):
                    if k == 0 and not (isinstance(t, int) and t < 2):
                        act.wait_ge(ht_stored[slot], 8 * t - (0 if slot else 8))
                    act.wait_ge(tp_filled, a_filled(t, 6 + k))
                    nc.scalar.activation(ht[:, slot, 0, HALF * k:HALF * k + HALF, :],
                                         tp[a_bank(6 + k)][:, :].rearrange("p (k c) -> p k c", c=P),
                                         ACT.Copy).then_inc(h_hi, 1)

                split_hi(act, G_ZA, range(2))
                for j in range(2):
                    act.wait_ge(tp_filled, j + 1)
                    nc.scalar.activation(ht[:, 0, 0, HALF * j:HALF * j + HALF, :],
                                         tp[j][:, :].rearrange("p (k c) -> p k c", c=P),
                                         ACT.Copy).then_inc(h_hi, 1)
                split_hi(act, G_ZA, range(2, KT))
                split_hi(act, G_ZG, range(KT))

                def step(t, p):
                    first = isinstance(t, int) and t == 0
                    second = isinstance(t, int) and t == 1
                    tail = isinstance(t, int) and t == T
                    cols = P if second else 2 * P
                    if not tail:
                        square_x(act, t + 1, 1 - p, 8 * t + (16 if p == 0 else 24))
                    if not first:
                        for k in range(2):
                            act.wait_ge(tp_filled, a_filled(t, k))
                            for odd in range(2):
                                rows, heads, src = q_views(k, odd)
                                nc.scalar.activation(q2t[rows, heads, :], src, ACT.Copy).then_inc(q_hi, 1)

                    def exp_z(j):
                        act.wait_ge(acc_filled, 4 * t + (j + 1))
                        if not first:
                            act.wait_ge(gate_ready, 2 * t + (j - 1))
                        nc.scalar.activation(ez[:, j, :], acc[j][:, :], ACT.Exp, scale=-1.0)\
                            .then_inc(e_ready, 1)
                        nc.scalar.activation(ez[:, 2 + j, :], acc[j][:, :], ACT.Copy)\
                            .then_inc(acc_drained[j], 1)

                    def exps(h0):
                        act.wait_ge(nmx_ready, 2 * t + (h0 // 4 - 1))
                        for h in range(h0, h0 + 4):
                            nc.scalar.activation(probs[:, h, 0:cols], probs[:, h, 0:cols], ACT.Exp,
                                                 bias=nmx[:, h:h + 1],
                                                 accum_out=psum_row[:, h:h + 1]).then_inc(exp_ready, 1)

                    def probs_t_out(j):
                        act.wait_ge(tp_filled, a_filled(t, 2 + j))
                        b = a_bank(2 + j)
                        src = tp[b][:, :].rearrange("p (h s c) -> p h s c", h=2, s=2)
                        nc.scalar.activation(probs_t[:, 2 * j:2 * j + 2, 0:cols // P, :], src[:, :, 0:cols // P, :],
                                             ACT.Copy).then_inc(tp_drained[b], 1)

                    last = isinstance(t, int) and t == T - 1
                    if not tail:
                        exp_z(0)
                    if first:
                        split_hi(act, G_KV, range(KT))
                    if last:
                        split_hi(act, G_QK, range(2))
                    if tail:
                        split_hi(act, G_V, range(4, 8))
                    if not first:
                        exps(0)
                    if last:
                        split_hi(act, G_QK, range(2, 4))
                    if not first:
                        exps(4)
                        act.wait_ge(sinkd_ready, t)
                        nc.scalar.activation(esink[:], sinkd[:], ACT.Exp).then_inc(esink_ready, 1)
                        probs_t_out(0)
                    if not tail:
                        exp_z(1)
                    if first:
                        split_hi(act, G_Q, range(KT))
                    if not first:
                        probs_t_out(2)
                    if last:
                        split_hi(act, G_QK, range(4, 8))
                    if not tail:
                        h_part_hi(t, 0, 1 - p)
                        h_part_hi(t, 1, 1 - p)
                        act.wait_ge(tp_filled, a_filled(t, 8))
                        nc.scalar.activation(k2t[:, 0, p, :, :], tp[a_bank(8)][:, 0:AKV * P].rearrange(
                            "p (h c) -> p h c", h=AKV), ACT.Copy).then_inc(k_hi, 1)
                        act.wait_ge(acc_filled, 4 * t + 4)
                        if not first:
                            act.wait_ge(tp_filled, a_filled(t, 1))
                        nc.scalar.activation(q_s[:], acc[1][:, :], ACT.Copy, scale=AD ** -0.5)\
                            .then_inc(acc_drained[1], 1)
                    if is_t(t, T - 2):
                        split_r_hi()
                    if last:
                        split_hi(act, G_V, range(4))

                steps(act, step)

                pass_a_done(act)

                def hi_part(t, k, dst, counter):
                    act.wait_ge(b_tp_filled, b_filled(t, k))
                    nc.scalar.activation(dst, tp[k % 2][:, :].rearrange("p (k c) -> p k c", c=P),
                                         ACT.Copy).then_inc(counter, 1)

                def square_y(t, p):
                    act.wait_ge(b_acc_drained[1], acc_prior(t - 1, 3) + 1)
                    nc.scalar.activation(junk_y[:], yb[:, p, :], ACT.Square,
                                         accum_out=ssy[:, p:p + 1]).then_inc(ssy_ready, 1)

                def step(t, p):
                    first, tail = is_t(t, 0), is_t(t, T)
                    if tail:
                        hi_part(t, 0, mix_t[:, 0, 0:HALF, :], mix_hi)
                    if not (isinstance(t, int) and t < 2):
                        square_y(t, p)
                    if not tail:
                        act.wait_ge(r_filled, 2 * t + 1)
                        nc.scalar.activation(r_t[0:2 * GR, :], rb[0:2 * GR, 0:P], ACT.Copy)\
                            .then_inc(rt_copied, 1)
                    if not first:
                        act.wait_ge(at_filled, t)
                        nc.scalar.activation(a_t[:, 0, :, :], at[0][:, 0:2 * P].rearrange(
                            "p (j c) -> p j c", c=P), ACT.Copy)
                        nc.scalar.activation(a_t[:, 1, :, :], at[1][:, 0:2 * P].rearrange(
                            "p (j c) -> p j c", c=P), ACT.Copy).then_inc(at_copied, 1)
                    if is_t(t, 1):
                        split_hi(act, G_OUT0, range(KT))
                    if not tail:
                        act.wait_ge(b_acc_filled, acc_use(t, 0) + 1)
                        nc.scalar.activation(qk[:, 0:GKW], acc[0][:, 0:GKW], ACT.Copy,
                                             scale=GK ** -0.5)
                        nc.scalar.activation(qk[:, GKW:], acc[0][:, GKW:], ACT.Copy)\
                            .then_inc(b_acc_drained[0], 1)
                        act.wait_ge(r_filled, 2 * t + 2)
                        if not first:
                            act.wait_ge(ls_ready, t)
                        y = rb[:, 256:512]
                        nc.scalar.activation(l_b[:], y, ACT.Abs).then_inc(l_ready, 1)
                        act.wait_ge(l_ready, 3 * t + 1)
                        nc.scalar.activation(l_b[:], l_b[:], ACT.Exp, scale=-1.0).then_inc(l_ready, 1)
                        act.wait_ge(l_ready, 3 * t + 2)
                        nc.scalar.activation(l_b[:], l_b[:], ACT.Ln, bias=1.0).then_inc(l_ready, 1)
                    if not (first or tail):
                        hi_part(t, 0, mix_t[:, 0, 0:HALF, :], mix_hi)
                    if not tail:
                        act.wait_ge(fsum_ready, t + 1)
                        nc.scalar.activation(fexp[:], fsum[:], ACT.Exp, scale=1.0 / GATE_NORM)\
                            .then_inc(fexp_ready, 1)
                    if not first:
                        act.wait_ge(o_filled, t)
                        if not is_t(t, 1):
                            act.wait_ge(ms4_ready, t - 1)
                        for h in range(GH):
                            nc.scalar.activation(junk_g[:, h, :], o_b[h % 2][:, h // 2, :], ACT.Square,
                                                 accum_out=ss4[:, h:h + 1]).then_inc(ss4_ready, 1)
                    if not tail:
                        act.wait_ge(b_mid, t + 1)
                        bb = b_b[:, :, :, :].rearrange("p j c i -> p j (c i)")
                        nc.scalar.activation(e_up[:], bb, ACT.Exp, scale=1.0 / GATE_NORM)
                        nc.scalar.activation(e_dn[:], bb, ACT.Exp, scale=-1.0 / GATE_NORM)\
                            .then_inc(decay_ready, 1)
                        if is_t(t, 1):
                            split_hi(act, G_OUT1, range(HALF))
                        act.wait_ge(b_acc_filled, acc_use(t, 1) + 1)
                        nc.scalar.activation(vb[:], acc[1][:, :], ACT.Copy).then_inc(b_acc_drained[1], 1)
                    if not first:
                        hi_part(t, 1, mix_t[:, 0, HALF:KT, :], mix_hi)
                    if is_t(t, 1):
                        split_hi(act, G_OUT1, range(HALF, KT))
                    if not tail:
                        act.wait_ge(b_tp_filled, b_filled(t, 3))
                        nc.scalar.activation(k_tok[:], tp[1][:, 0:2 * P].rearrange(
                            "p (j c) -> p j c", c=P), ACT.Copy).then_inc(b_tp_drained[1], 1)

                steps(act, step)
                square_y(T + 1, 1)

            @block.vector
            def _(dve):
                nc.vector.memset(line, NEG).then_inc(line_set, 1)
                nc.vector.memset(zline, 0.0).then_inc(line_set, 1)
                scale_x(dve, 0, 0)
                split_lo(dve, G_ZA, range(2))
                for j in range(2):
                    dve.wait_ge(h_hi, j + 1)
                    nc.vector.tensor_tensor(ht[:, 0, 1, HALF * j:HALF * j + HALF, :],
                                            tp[j][:, :].rearrange("p (k c) -> p k c", c=P),
                                            ht[:, 0, 0, HALF * j:HALF * j + HALF, :].bitcast(F32),
                                            ALU.subtract).then_inc(tp_drained[j], 1)
                split_lo(dve, G_ZA, range(2, KT))
                split_lo(dve, G_ZG, range(KT))

                def step(t, p):
                    first = isinstance(t, int) and t == 0
                    second = isinstance(t, int) and t == 1
                    tail = isinstance(t, int) and t == T
                    cols = P if second else 2 * P

                    def bias_max(h0):
                        for h in range(h0, h0 + 4):
                            dve.wait_ge(sc_filled, 4 * t + (h // 2 - 3))
                            hold(dve)
                            b = (h // 2) % 2
                            src = sc[b][:, (h % 2) * 2 * P:(h % 2) * 2 * P + cols]
                            last = nc.vector.tensor_tensor_reduce(
                                probs[:, h, 0:cols], src, bias[:, h, p * P:p * P + cols], 1.0, sink[:, h:h + 1],
                                ALU.add, ALU.max, mx[:, h:h + 1])
                            if h % 2:
                                last.then_inc(sc_drained[b], 1)
                        dve.wait_ge(sc_drained[0], 2 * t + (h0 // 4 - 1))
                        dve.wait_ge(sc_drained[1], 2 * t + (h0 // 4 - 1))
                        nc.vector.tensor_scalar(nmx[:, h0:h0 + 4], mx[:, h0:h0 + 4], -1.0, None,
                                                ALU.mult).then_inc(nmx_ready, 1)

                    def recip(j, c, tile=t):
                        dve.wait_ge(e1_ready, 2 * tile + (j + 1))
                        nc.vector.reciprocal(ez[:, j, 256 * c:256 * c + 256],
                                             ez[:, j, 256 * c:256 * c + 256]).then_inc(rec_ready, 1)

                    def probs_t_out(j):
                        dve.wait_ge(tp_filled, a_filled(t, 2 + j))
                        b = a_bank(2 + j)
                        src = tp[b][:, :].rearrange("p (h s c) -> p h s c", h=2, s=2)
                        nc.vector.tensor_copy(probs_t[:, 2 * j:2 * j + 2, 0:cols // P, :],
                                              src[:, :, 0:cols // P, :]).then_inc(tp_drained[b], 1)

                    if not tail:
                        scale_x(dve, t + 1, 1 - p)
                    last_tile = isinstance(t, int) and t == T - 1
                    if first:
                        split_lo(dve, G_KV, range(KT))
                        split_lo(dve, G_Q, range(KT))
                    if not first:
                        for k in range(2):
                            for odd in range(2):
                                dve.wait_ge(q_hi, 4 * t + (2 * k + odd - 3))
                                rows, heads, src = q_views(k, odd)
                                other = slice(AD - AD * odd, 2 * AD - AD * odd)
                                last = nc.vector.tensor_tensor(q2t[other, heads, :], src,
                                                               q2t[rows, heads, :].bitcast(F32), ALU.subtract)
                            last.then_inc(tp_drained[a_bank(k)], 1)
                        if second:
                            recip(1, 0, 0)
                            recip(1, 1, 0)
                        if tail:
                            split_lo(dve, G_V, range(4, 6))
                        if second:
                            dve.wait_ge(bias_loaded, 16 * AH)
                        bias_max(0)
                    if last_tile:
                        split_lo(dve, G_QK, range(2))
                    if tail:
                        split_lo(dve, G_V, range(6, 8))
                    if not (first or tail):
                        recip(0, 0)
                    if not first:
                        bias_max(4)
                        dve.wait_ge(nmx_ready, 2 * t)
                        nc.vector.tensor_tensor(sinkd[:], sink[:], nmx[:], ALU.add).then_inc(sinkd_ready, 1)
                    if last_tile:
                        split_lo(dve, G_QK, range(2, 4))
                    if not (first or tail):
                        recip(0, 1)
                    if not first:
                        probs_t_out(1)
                        dve.wait_ge(exp_ready, 8 * t)
                        dve.wait_ge(esink_ready, t)
                        nc.vector.tensor_tensor(den[:], psum_row[:], esink[:], ALU.add).then_inc(den_ready, 1)
                        dve.wait_ge(den_ready, t)
                        nc.vector.reciprocal(rden[:], den[:]).then_inc(rden_ready, 1)
                        probs_t_out(3)
                    if last_tile:
                        split_lo(dve, G_QK, range(4, 8))
                    if not tail:
                        if not first:
                            recip(1, 0)
                        dve.wait_ge(acc_filled, 4 * t + 3)
                        if not first:
                            dve.wait_ge(tp_filled, a_filled(t, 0))
                        for c in range(2):
                            nc.vector.tensor_copy(k_s[:, :, c, :], acc[0][:, 0:AKW].rearrange(
                                "p (h d) -> p h d", d=AD))
                        if not first:
                            dve.wait_ge(oa_filled, t)
                        nc.vector.tensor_copy(va[:, p, :, :], acc[0][:, AKW:2 * AKW].rearrange(
                            "p (h d) -> p h d", d=AD)).then_inc(acc_drained[0], 1)
                    if not first:
                        dve.wait_ge(oa_filled, t)
                        dve.wait_ge(gate_scaled, t)
                        if not second:
                            dve.wait_ge(mixa_stored, 16 * t - 16)
                        nc.vector.tensor_tensor(mixa[:, 1 - p, :], oa[:, :], gate_a[:, 1 - p, :],
                                                ALU.mult).then_inc(mixa_ready, 1)
                    if not tail:
                        for k in range(2):
                            dve.wait_ge(h_hi, 2 * t + (3 + k))
                            nc.vector.tensor_tensor(
                                ht[:, 1 - p, 1, HALF * k:HALF * k + HALF, :],
                                tp[a_bank(6 + k)][:, :].rearrange("p (k c) -> p k c", c=P),
                                ht[:, 1 - p, 0, HALF * k:HALF * k + HALF, :].bitcast(F32),
                                ALU.subtract).then_inc(tp_drained[a_bank(6 + k)], 1)
                        if first:
                            recip(0, 0)
                            recip(0, 1)
                        else:
                            recip(1, 1)
                        dve.wait_ge(k_hi, t + 1)
                        nc.vector.tensor_tensor(k2t[:, 1, p, :, :], tp[a_bank(8)][:, 0:AKV * P].rearrange(
                            "p (h c) -> p h c", h=AKV), k2t[:, 0, p, :, :].bitcast(F32), ALU.subtract)\
                            .then_inc(tp_drained[a_bank(8)], 1)
                    if second:
                        dve.wait_ge(bias_widened, 1)
                    if is_t(t, T - 2):
                        split_r_lo()
                    if last_tile:
                        split_lo(dve, G_V, range(4))

                steps(dve, step)

                pass_a_done(dve)
                dve.wait_ge(b_set, 2)

                def lo_part(t, k, dst, hi, counter, count):
                    dve.wait_ge(counter, count)
                    nc.vector.tensor_tensor(dst, tp[k % 2][:, :].rearrange("p (k c) -> p k c", c=P),
                                            hi.bitcast(F32), ALU.subtract).then_inc(b_tp_drained[k % 2], 1)

                def finish(t, p):
                    if is_t(t, 2):
                        dve.wait_ge(gain_loaded_b, 16)
                    dve.wait_ge(rsy_ready, t - 1)
                    nc.vector.scalar_tensor_tensor(out=yb[:, p, :], in0=yb[:, p, :], scalar=rsy[:, p:p + 1],
                                                   in1=gain_row[:], op0=ALU.mult, op1=ALU.mult)\
                        .then_inc(y_scaled, 1)

                def step(t, p):
                    first, tail = is_t(t, 0), is_t(t, T)
                    if tail:
                        lo_part(t, 0, mix_t[:, 1, 0:HALF, :], mix_t[:, 0, 0:HALF, :], mix_hi, 2 * t - 1)
                    if not (isinstance(t, int) and t < 2):
                        finish(t, p)
                    if not (first or tail):
                        dve.wait_ge(u_filled, t)
                        dve.wait_ge(state_ready, 2 * t)
                        nc.vector.tensor_tensor(state_x[:], u_b, state[:], ALU.add).then_inc(x_state, 1)
                        if is_t(t, 1):
                            split_lo(dve, G_OUT0, range(KT))
                    if not tail:
                        dve.wait_ge(l_ready, 3 * t + 3)
                        nc.vector.scalar_tensor_tensor(out=ls_b[:], in0=rb[:, 256:512], scalar=0.0,
                                                       in1=l_b[:], op0=ALU.min, op1=ALU.subtract)\
                            .then_inc(ls_ready, 1)
                        dve.wait_ge(ls_ready, t + 1)
                        if not first:
                            dve.wait_ge(decay_ready, t)
                        nc.vector.tensor_tensor_scan(
                            b_b[:].rearrange("p j c i -> p (j c i)"), scan_mask[:], ls_b[:], 0.0,
                            ALU.mult, ALU.add).then_inc(b_scanned, 1)
                        dve.wait_ge(b_scanned, t + 1)
                        nc.vector.tensor_copy(bl[:, p, :, :], b_b[:, :, :, GC - 1]).then_inc(bl_ready, 1)
                        dve.wait_ge(bl_ready, t + 1)
                        nc.vector.tensor_tensor(fsum[:], bl[:, p, :, 0], bl[:, 1 - p, :, 1], ALU.add)\
                            .then_inc(fsum_ready, 1)
                        nc.vector.tensor_tensor(b_b[:, :, 0, :], b_b[:, :, 0, :],
                                                bl[:, p, :, 0:1].to_broadcast((P, 2, GC)),
                                                ALU.subtract).then_inc(b_mid, 1)
                    if not (first or tail):
                        lo_part(t, 0, mix_t[:, 1, 0:HALF, :], mix_t[:, 0, 0:HALF, :], mix_hi, 2 * t - 1)
                    if not first:
                        dve.wait_ge(o_filled, t)
                    if not tail:
                        dve.wait_ge(fexp_ready, t + 1)
                        if not first:
                            dve.wait_ge(x_state, t)
                        for j in range(2):
                            nc.vector.tensor_scalar(state[:, j, :], state_x[:, j, :], fexp[:, j:j + 1], None,
                                                    ALU.mult).then_inc(state_ready, 1)
                    if is_t(t, 1):
                        split_lo(dve, G_OUT1, range(HALF))
                    if not first:
                        dve.wait_ge(mixg_scaled, t)
                        for o in range(2):
                            last = nc.vector.tensor_tensor(mix_g[:, o], o_b[o], mix_g[:, o], ALU.mult)
                        last.then_inc(mix_ready, 1)
                        lo_part(t, 1, mix_t[:, 1, HALF:KT, :], mix_t[:, 0, HALF:KT, :], mix_hi, 2 * t)
                    if not tail:
                        dve.wait_ge(decay_ready, t + 1)
                        dve.wait_ge(b_tp_filled, b_filled(t, 2))
                        nc.vector.tensor_tensor(q_dec[:], tp[0][:, 0:2 * P].rearrange(
                            "p (j c) -> p j c", c=P), e_up[:], ALU.mult)
                        nc.vector.tensor_tensor(k_dec[:], tp[0][:, 2 * P:4 * P].rearrange(
                            "p (j c) -> p j c", c=P), e_dn[:], ALU.mult).then_inc(b_tp_drained[0], 1)
                    if is_t(t, 1):
                        split_lo(dve, G_OUT1, range(HALF, KT))
                    if not first:
                        for g in range(2):
                            dve.wait_ge(b_acc_filled, acc_use(t, 2 + g) + 1)
                            if g == 0:
                                dve.wait_ge(y_loaded[1 - p], 8 * t + (8 if p else 0))
                            half_y = yb[:, 1 - p, 512 * g:512 * g + 512]
                            nc.vector.tensor_tensor(half_y, acc[g][:, :], half_y, ALU.add)\
                                .then_inc(b_acc_drained[g], 1)

                steps(dve, step)
                finish(T + 1, 1)

            @block.tensor
            def _(pe):
                def h_transposes(t, k, slot, xslot):
                    b = a_bank(6 + k)
                    for c in range(4):
                        kt = HALF * k + c
                        last = nc.tensor.transpose(tp[b][:, c * P:(c + 1) * P],
                                                   xb[:, xslot, kt * P:(kt + 1) * P], ident[:])
                    last.then_inc(tp_filled, 1)

                def project_b(b, g, p, kts, unsplit):
                    for kt in kts:
                        if unsplit:
                            pe.wait_ge(w_lo, split_count(g, kt))
                        for i, (a, w) in enumerate(((0, 0), (0, 1), (1, 0))):
                            last = nc.tensor.matmul(acc[b][:, :], ht[:, p, a, kt, :],
                                                    w_home[g][:, w, kt, :],
                                                    start=(kt == 0 and i == 0), stop=(kt == KT - 1 and i == 2))
                    if KT - 1 in kts:
                        last.then_inc(b_acc_filled, 1)

                def project_r(p):
                    for kt in range(KT):
                        for s in range(2):
                            last = nc.tensor.matmul(rb[0:2 * GR, 0:P], w_r[:, kt, :], ht[:, p, s, kt, :],
                                                    start=(kt == 0 and s == 0), stop=(kt == KT - 1 and s == 1))
                    last.then_inc(r_filled, 1)

                pe.wait_ge(ident_set, 2)
                pe.wait_ge(h_ready, 1)
                for j in range(2):
                    for c in range(4):
                        kt = HALF * j + c
                        last = nc.tensor.transpose(tp[j][:, c * P:(c + 1) * P],
                                                   xb[:, 0, kt * P:(kt + 1) * P], ident[:])
                    last.then_inc(tp_filled, 1)

                def step(t, p):
                    first = isinstance(t, int) and t == 0
                    second = isinstance(t, int) and t == 1
                    tail = isinstance(t, int) and t == T

                    def project(g, halves):
                        b, n = g % 2, G_COLS[g][1]
                        if 0 in halves and not (first and g < 2):
                            pe.wait_ge(acc_drained[b], 2 * t + g // 2)
                        for half_ in halves:
                            for kt in range(HALF * half_, HALF * half_ + HALF):
                                if first:
                                    pe.wait_ge(w_lo, split_count(g, kt))
                                hi, lo = ht[:, p, 0, kt, :], ht[:, p, 1, kt, :]
                                for i, (a, w) in enumerate(((hi, 0), (hi, 1), (lo, 0))):
                                    last = nc.tensor.matmul(acc[b][:, 0:n], a, w_home[g][:, w, kt, :],
                                                            start=(kt == 0 and i == 0),
                                                            stop=(kt == KT - 1 and i == 2))
                        if 1 in halves:
                            last.then_inc(acc_filled, 1)

                    def q_transposes(k):
                        b = a_bank(k)
                        pe.wait_ge(tp_drained[b], a_prior(t, k))
                        pe.wait_ge(acc_drained[1], 2 * t)
                        for c in range(2):
                            last = nc.tensor.transpose(tp[b][:, c * P:(c + 1) * P],
                                                       q_s[:, (2 * k + c) * P:(2 * k + c + 1) * P], ident[:])
                        last.then_inc(tp_filled, 1)

                    def scores(h0):
                        a_data(pe, t, h0 // 4)
                        if h0 == 0:
                            a_data(pe, t - 1, 8)
                        for h in range(h0, h0 + 4):
                            b = (h // 2) % 2
                            if h % 2 == 0 and not (second and h0 == 0):
                                pe.wait_ge(sc_drained[b], 2 * t + (h0 // 4 - 2))
                            slots = 1 if second else 2
                            for w in range(2):
                                last = nc.tensor.matmul(
                                    sc[b][:, (h % 2) * 2 * P:(h % 2) * 2 * P + slots * P],
                                    q2t[:, h, :], k2t[:, w, 0:slots, h // AG, :],
                                    start=(w == 0), stop=(w == 1))
                            if h % 2:
                                last.then_inc(sc_filled, 1)

                    def probs_transposes(j):
                        b = a_bank(2 + j)
                        pe.wait_ge(tp_drained[b], a_prior(t, 2 + j))
                        pe.wait_ge(exp_ready, 8 * t + (2 * j - 6))
                        for h in range(2):
                            for s in range(1 if second else 2):
                                last = nc.tensor.transpose(tp[b][:, (2 * h + s) * P:(2 * h + s + 1) * P],
                                                           probs[:, 2 * j + h, s * P:(s + 1) * P], ident[:])
                        last.then_inc(tp_filled, 1)

                    def attend(h0):
                        if h0 == 0 and not second:
                            pe.wait_ge(mixa_ready, t - 1)
                        if h0 == 0:
                            pe.wait_ge(acc_drained[0], 2 * t)
                        for h in range(h0, h0 + 4):
                            if h % 2 == 0:
                                a_data(pe, t, 2 + h // 2)
                            slots = 1 if second else 2
                            for s in range(slots):
                                last = nc.tensor.matmul(oa[:, h * AD:(h + 1) * AD], probs_t[:, h, s, :],
                                                        va[:, s, h // AG, :],
                                                        start=(s == 0), stop=(s == slots - 1))
                        if h0 == 4:
                            last.then_inc(oa_filled, 1)

                    if tail:
                        for k in range(2):
                            a_data(pe, t - 1, 6 + k)
                        pe.wait_ge(acc_drained[0], 2 * T)
                        project_b(0, G_QK, 0, range(HALF), True)
                        q_transposes(0)
                        q_transposes(1)
                        project_b(0, G_QK, 0, range(HALF, KT), True)
                        scores(0)
                        project_b(1, G_V, 0, range(HALF), True)
                        scores(4)
                        probs_transposes(0)
                        probs_transposes(1)
                        project_b(1, G_V, 0, range(HALF, KT), True)
                        probs_transposes(2)
                        probs_transposes(3)
                        pe.wait_ge(tp_drained[2], 3 * T)
                        pe.wait_ge(w_r_lo, KT)
                        project_r(0)
                        attend(0)
                        attend(4)
                        return
                    if first:
                        pe.wait_ge(tp_drained[0], 1)
                        pe.wait_ge(tp_drained[1], 1)
                    else:
                        for k in range(2):
                            a_data(pe, t - 1, 6 + k)
                    project(G_ZA, (0,))
                    if not first:
                        q_transposes(0)
                        q_transposes(1)
                    project(G_ZA, (1,))
                    if not first:
                        scores(0)
                    project(G_ZG, (0,))
                    if not first:
                        scores(4)
                    project(G_ZG, (1,))
                    if not first:
                        probs_transposes(0)
                        probs_transposes(1)
                    project(G_KV, (0,))
                    if not first:
                        probs_transposes(2)
                        probs_transposes(3)
                        attend(0)
                    project(G_KV, (1,))
                    if not first:
                        attend(4)
                    pe.wait_ge(h_ready, t + 2)
                    for k in range(2):
                        pe.wait_ge(tp_drained[a_bank(6 + k)], a_prior(t, 6 + k))
                        h_transposes(t, k, 1 - p, 1 - p)
                    project(G_Q, (0, 1) if first else (0,))
                    pe.wait_ge(tp_drained[a_bank(8)], a_prior(t, 8))
                    pe.wait_ge(acc_drained[0], 2 * t + 2)
                    for h in range(AKV):
                        last = nc.tensor.transpose(tp[a_bank(8)][:, h * P:(h + 1) * P],
                                                   k_s[:, h, :, :].rearrange("p c d -> p (c d)"), ident[:])
                    last.then_inc(tp_filled, 1)
                    if not first:
                        project(G_Q, (1,))

                steps(pe, step)

                def step(t, p):
                    first, second, tail = is_t(t, 0), is_t(t, 1), is_t(t, T)
                    def acc_free(g):
                        if not (first or (second and acc_prior(t, g) < 1)):
                            pe.wait_ge(b_acc_drained[g % 2], acc_prior(t, g))

                    def output(g, kts):
                        if 0 in kts:
                            acc_free(2 + g)
                        for kt in kts:
                            if second:
                                pe.wait_ge(w_lo, split_count(G_OUT0 + g, kt))
                            for i, (a, w) in enumerate(((0, 0), (0, 1), (1, 0))):
                                last = nc.tensor.matmul(acc[g][:, :], mix_t[:, a, kt, :],
                                                        w_home[G_OUT0 + g][:, w, kt, :],
                                                        start=(kt == 0 and i == 0),
                                                        stop=(kt == KT - 1 and i == 2))
                        if KT - 1 in kts:
                            last.then_inc(b_acc_filled, 1)

                    def mix_transposes():
                        tp_free(0)
                        pe.wait_ge(mix_loaded, 16 * t)
                        for c in range(HALF):
                            last = nc.tensor.transpose(tp[0][:, c * P:(c + 1) * P],
                                                       mix[:, c * P:(c + 1) * P], ident[:])
                        last.then_inc(b_tp_filled, 1)

                    def tp_free(k):
                        if not (first and k >= 2):
                            pe.wait_ge(b_tp_drained[k % 2], b_prior(t, k))

                    if first:
                        pe.wait_ge(mixa_ready, T)
                        for b in range(3):
                            pe.wait_ge(tp_drained[b], 3 * T + (1, 1, 0)[b])
                    if not tail:
                        if not (first or second):
                            pe.wait_ge(ht_loaded[p], 8 * t + (0 if p == 0 else 8))
                        if not (first or second):
                            pe.wait_ge(ls_ready, t)
                            project_r(p)
                    if tail:
                        mix_transposes()
                    if not first:
                        b_data(pe, t - 1, 2)
                        if not second:
                            pe.wait_ge(x_state, t - 1)
                            pe.wait_ge(at_copied, t - 1)
                            pe.wait_ge(mix_ready, t - 1)
                        for o in range(2):
                            rows = slice(GK * o, GK * o + GK)
                            for j in range(2):
                                last = nc.tensor.matmul(at[o][:, j * P:(j + 1) * P], k_dec[rows, j, :],
                                                        q_dec[rows, j, :], start=True, stop=True)
                        last.then_inc(at_filled, 1)
                    if not (first or second or tail):
                        acc_free(0)
                        project_b(0, G_QK, p, range(HALF), False)
                    if not (first or tail):
                        b_data(pe, t - 1, 3)
                        acc_data(pe, t - 1, 1)
                        pe.wait_ge(at_copied, t)
                        for h in range(GH):
                            rows = slice(GK * (h % 2), GK * (h % 2) + GK)
                            last = nc.tensor.matmul(u_b[rows, h // 2, :], k_tok[:, h // 2, rows],
                                                    vb[:, h * GV:(h + 1) * GV], start=True, stop=True)
                        last.then_inc(u_filled, 1)
                    if tail:
                        acc_data(pe, t - 1, 1)
                    if not (first or tail):
                        project_b(0, G_QK, p, range(HALF, KT), False)
                    if not tail:
                        pe.wait_ge(rt_copied, t + 1)
                        for j in range(2):
                            last = nc.tensor.matmul(rb[:, 256 + j * P:256 + (j + 1) * P],
                                                    w_up[:, j * P:(j + 1) * P], r_t[:],
                                                    start=True, stop=True)
                        last.then_inc(r_filled, 1)
                    if tail:
                        b_data(pe, t, 0)
                        output(0, range(HALF))
                    if not first:
                        pe.wait_ge(at_masked, t)
                        pe.wait_ge(state_ready, 2 * t)
                        for h in range(GH):
                            rows = slice(GK * (h % 2), GK * (h % 2) + GK)
                            dst = o_b[h % 2][:, h // 2, :]
                            nc.tensor.matmul(dst, q_dec[rows, h // 2, :], state[rows, h // 2, :],
                                             start=True, stop=False)
                            last = nc.tensor.matmul(dst, a_t[:, h % 2, h // 2, :],
                                                    vb[:, h * GV:(h + 1) * GV], start=False, stop=True)
                        last.then_inc(o_filled, 1)
                        if tail:
                            output(1, range(HALF))
                        else:
                            mix_transposes()
                    if not (first or tail):
                        acc_free(1)
                        project_b(1, G_V, p, range(KT), False)
                    if not first:
                        tp_free(1)
                        pe.wait_ge(mix_ready, t)
                        for c in range(HALF):
                            last = nc.tensor.transpose(tp[1][:, c * P:(c + 1) * P],
                                                       mix[:, AW + c * P:AW + (c + 1) * P], ident[:])
                        last.then_inc(b_tp_filled, 1)
                    if not tail:
                        tp_free(2)
                        acc_data(pe, t, 0)
                        for c in range(4):
                            last = nc.tensor.transpose(tp[0][:, c * P:(c + 1) * P],
                                                       qk[:, c * P:(c + 1) * P], ident[:])
                        last.then_inc(b_tp_filled, 1)
                    if not (first or tail):
                        b_data(pe, t, 0)
                        output(0, range(HALF))
                    if not first:
                        b_data(pe, t, 1)
                        output(0, range(HALF, KT))
                    if first:
                        pe.wait_ge(ht_loaded[1], 16)
                        pe.wait_ge(b_acc_drained[0], 1)
                        project_b(0, G_QK, 1, range(HALF), False)
                        pe.wait_ge(ls_ready, 1)
                        project_r(1)
                    if not tail:
                        tp_free(3)
                        b_data(pe, t, 2)
                        for j in range(2):
                            last = nc.tensor.transpose(tp[1][:, j * P:(j + 1) * P], k_dec[:, j, :], ident[:])
                        last.then_inc(b_tp_filled, 1)
                    if not first:
                        output(1, range(HALF, KT) if tail else range(KT))

                steps(pe, step)


_INS = ["x", "norm_gain", "w_in", "w_gate_up", "b_gate", "rel_bias", "sinks", "gla_norm_gain", "w_out",
        "final_norm_gain"]


def kernel(**inputs):
    import numpy as _np
    import concourse.bacc as _bacc
    from concourse import mybir as _mybir
    from concourse.bass_utils import run_bass_kernel_spmd as _run

    nc = _bacc.Bacc("TRN2", target_bir_lowering=False, num_devices=1, dynamic_dma_scratch_size=1024)
    arrays, args = {}, []
    for name in _INS:
        a = _np.ascontiguousarray(inputs[name])
        arrays[f"in_{name}_dram"] = a
        args.append(nc.dram_tensor(f"in_{name}_dram", a.shape, _mybir.dt.from_np(a.dtype),
                                   kind="ExternalInput").ap())
    args.append(nc.dram_tensor("out_0_dram", (1, S, D), F32, kind="ExternalOutput").ap())
    hybrid_block(nc, *args)
    r = _run(nc, [arrays], core_ids=[0])
    return r.results[0]["out_0_dram"]
```

```python
from contextlib import ExitStack

import numpy as np

import concourse.bass as bass
from concourse import mybir

F32 = mybir.dt.float32
F32R = mybir.dt.float32r
BF16 = mybir.dt.bfloat16
ALU = mybir.AluOpType
ACT = mybir.ActivationFunctionType

P = 128
D = 1024
S = 2048
T = S // P
KT = D // P
EPS = 1e-6
NEG = -1e30

AH, AKV, AD = 8, 2, 64
AG = AH // AKV
AW, AKW = AH * AD, AKV * AD
NUM_BUCKETS, MAX_DISTANCE, WINDOW = 32, 128, 128
GH, GK, GV, GR, GC = 4, 64, 128, 16, 64
GKW, GW = GH * GK, GH * GV
GATE_NORM = 16.0

C_Q, C_KV = 0, AW
C_ZA = C_KV + 2 * AKW
C_QK = C_ZA + AW
C_V = C_QK + 2 * GKW
C_ZG = C_V + GW
C_R = C_ZG + GW
N_IN = C_R + GR

HALF = KT // 2
NW = 512

G_ZA, G_ZG, G_KV, G_Q, G_QK, G_V, G_OUT0, G_OUT1 = range(8)
G_COLS = ((C_ZA, AW), (C_ZG, GW), (C_KV, 2 * AKW), (C_Q, AW), (C_QK, 2 * GKW), (C_V, GW), (0, NW), (NW, NW))


def split_count(g, kt):
    return KT * g + kt + 1


def bucket(n):
    exact = NUM_BUCKETS // 2
    if n < exact:
        return n
    large = exact + int(np.log(n / exact) / np.log(MAX_DISTANCE / exact) * (NUM_BUCKETS - exact))
    return min(large, NUM_BUCKETS - 1)


def bucket_runs():
    runs = []
    for j in range(P, 2 * P):
        b = bucket(2 * P - 1 - j)
        if runs and runs[-1][2] == b:
            runs[-1][1] = j + 1
        else:
            runs.append([j, j + 1, b])
    return runs


def a_filled(t, k):
    return 9 * t + (k - 3)


def a_bank(k):
    return (k + 2) % 3


def a_prior(t, k):
    return 3 * t + (k - 4) // 3


def b_filled(t, k):
    return 3 * t + (k - 1)


def b_prior(t, k):
    return t if k == 2 else 2 * t + (k - 3) // 2


def acc_use(t, g):
    if isinstance(t, int) and t == 0:
        return g
    if isinstance(t, int) and t == T:
        return 4 * t - 4 + g
    return 4 * t + (g - 2)


def acc_prior(t, g):
    if isinstance(t, int) and t == 0:
        return 0
    if isinstance(t, int) and t == T:
        return 2 * t + (g - 4) // 2
    return 2 * t + (g // 2 - 1)


def is_t(t, n):
    return isinstance(t, int) and t == n


def steps(eng, body):
    body(0, 0)
    body(1, 1)
    with eng.Fori(2, T - 2, 2) as t:
        body(t, 0)
        body(t + 1, 1)
    for t in range(T - 2, T + 1):
        body(t, t % 2)


def hybrid_block(nc, x, norm_gain, w_in, w_gate_up, b_gate, rel_bias, sinks, gla_norm_gain, w_out,
                 final_norm_gain, out):
    x_t = x.rearrange("o (t p) d -> (o t) p d", p=P)
    out_t = out.rearrange("o (t p) d -> (o t) p d", p=P)
    w_in_k = w_in.rearrange("l (k p) n -> (l p) k n", p=P)
    w_out_h = w_out.rearrange("l (h d) n -> (l d) h n", d=AD)
    w_out_k = w_out.rearrange("l (k p) n -> (l p) k n", p=P)
    mix_dram = nc.dram_tensor("mix_scratch", (T, P, D), F32).ap()
    ht_dram = nc.dram_tensor("ht_scratch", (T, P, 2 * KT * P), F32).ap()
    line_dram = nc.dram_tensor("bias_lines", (AH, P, 3 * P), F32)

    with ExitStack() as ctx:
        def sb(name, shape, dt=F32):
            return ctx.enter_context(nc.sbuf_tensor(name, shape, dt))

        def bank(name):
            return ctx.enter_context(nc.psum_tensor(name, [P, 512], F32))

        def sem(name):
            return ctx.enter_context(nc.semaphore(name))

        w_block = [sb(f"w_block{i}", [P, 2, KT, NW], F32R) for i in range(3)]
        xb = sb("xb", [P, 2, D])
        ht = sb("ht", [P, 2, 2, KT, P], F32R)
        junk = sb("junk", [P, D], BF16)
        ez = sb("ez", [P, 4, AW])
        raw_out = ez[:, :, :].rearrange("p (i m) (c n) -> p i (m c) n", i=2, n=2 * AKW)
        ident = sb("ident", [P, P])
        gain_col = sb("gain_col", [P, KT])
        gla_gain_col = sb("gla_gain_col", [P, 1])
        half = sb("half", [P, AH])
        ss = sb("ss", [P, 2])
        ms = sb("ms", [P, 2])
        rstd = sb("rstd", [P, 2])
        r_all = sb("r_all", [P, T, GR])
        stage_r = r_all[:, T - KT:T, :]
        r_in = sb("r_in", [P, 2, GR])
        r_t = sb("r_t", [GR + 1, P])
        w_up = sb("w_up", [GR + 1, GKW])
        sink = sb("sink", [P, AH])
        mx = sb("mx", [P, AH])
        nmx = sb("nmx", [P, AH])
        sinkd = sb("sinkd", [P, AH])
        esink = sb("esink", [P, AH])
        psum_row = sb("psum_row", [P, AH])
        den = sb("den", [P, AH])
        rden = sb("rden", [P, AH])
        rel_t = sb("rel_t", [AH, NUM_BUCKETS])

        x_loaded = [sem(f"x_loaded{i}") for i in range(2)]
        const_loaded = sem("const_loaded")
        gain_loaded = sem("gain_loaded")
        const_set = sem("const_set")
        held = sem("held")
        ident_set = sem("ident_set")
        line_set = sem("line_set")
        line_stored = sem("line_stored")
        bias_loaded = sem("bias_loaded")
        bias_widened = sem("bias_widened")
        raw_loaded = [sem(f"raw_loaded{i}") for i in range(HALF)]
        raw_out_loaded = [sem(f"raw_out_loaded{i}") for i in range(2)]
        raw_r_loaded = sem("raw_r_loaded")
        r_gained = sem("r_gained")
        w_hi = sem("w_hi")
        w_lo = sem("w_lo")
        w_r_hi = sem("w_r_hi")
        w_r_lo = sem("w_r_lo")
        ss_ready = sem("ss_ready")
        ms_ready = sem("ms_ready")
        rstd_ready = sem("rstd_ready")
        h_ready = sem("h_ready")
        h_hi = sem("h_hi")
        ht_stored = [sem(f"ht_stored{i}") for i in range(2)]
        ht_loaded = [sem(f"ht_loaded{i}") for i in range(2)]

        def settle(eng):
            eng.wait_ge(ident_set, 2)

        def hold(eng):
            eng.sem_inc(held, 1)

        def square_x(act, n, slot, loads):
            act.wait_ge(x_loaded[slot], loads)
            nc.scalar.activation(junk[:], xb[:, slot, :], ACT.Square,
                                 accum_out=ss[:, slot:slot + 1]).then_inc(ss_ready, 1)

        def rstd_x(pool, n, slot):
            pool.wait_ge(ss_ready, n + 1)
            hold(pool)
            nc.gpsimd.tensor_scalar(ms[:, slot:slot + 1], ss[:, slot:slot + 1], 1.0 / D, EPS,
                                    ALU.mult, ALU.add).then_inc(ms_ready, 1)
            pool.wait_ge(ms_ready, n + 1)
            nc.gpsimd.tensor_tensor(rstd[:, slot:slot + 1], ms[:, slot:slot + 1], half[:, 0:1],
                                    ALU.pow).then_inc(rstd_ready, 1)

        def scale_x(dve, n, slot):
            dve.wait_ge(rstd_ready, n + 1)
            nc.vector.tensor_scalar(xb[:, slot, :], xb[:, slot, :], rstd[:, slot:slot + 1], None,
                                    ALU.mult).then_inc(h_ready, 1)

        def raw_pair(g, i):
            if g == G_OUT1:
                return raw_out[:, i % 2]
            return raw_w[:, i]

        def load_raw(sp, g, i):
            c0, n = G_COLS[g]
            if g == G_OUT1:
                if i >= 2:
                    sp.wait_ge(w_lo, split_count(g, 2 * i - 3))
                else:
                    sp.wait_ge(gate_ready, 2 * T)
                loaded = raw_out_loaded[i % 2]
            else:
                if g > 0:
                    sp.wait_ge(w_lo, split_count(g - 1, 2 * i + 1))
                loaded = raw_loaded[i]
            src = w_out_k if g >= G_OUT0 else w_in_k
            pieces = n // (2 * AKW)
            if g >= G_OUT0 and i < 2:
                for r in range(2):
                    for kv in range(AKV):
                        sp.dma_start(raw_pair(g, i)[AD * kv:AD * kv + AD, pieces * r:pieces * r + pieces, :],
                                     w_out_h[:, AG * kv + 2 * i + r, c0:c0 + n]
                                     .rearrange("p (c n) -> p c n", n=2 * AKW)).then_inc(loaded, 16)
                return
            for r in range(2):
                sp.dma_start(raw_pair(g, i)[:, pieces * r:pieces * r + pieces, :],
                             src[:, 2 * i + r, c0:c0 + n].rearrange("p (c n) -> p c n", n=2 * AKW))\
                  .then_inc(loaded, 16)

        def split_views(g, kt):
            pieces = G_COLS[g][1] // (2 * AKW)
            raw = raw_pair(g, kt // 2)[:, pieces * (kt % 2):pieces * (kt % 2) + pieces, :]
            dst = w_home[g][:, :, kt, 0:G_COLS[g][1]].rearrange("p s (c n) -> p s c n", n=2 * AKW)
            if g < G_OUT0:
                gain = gain_col[:, kt:kt + 1]
            else:
                gain = gla_gain_col[:, 0:1] if kt >= HALF else 1.0
            return raw, dst, gain

        def split_hi(act, g, kts):
            for kt in kts:
                raw, dst, gain = split_views(g, kt)
                if g >= G_QK and kt == 0:
                    act.wait_ge(acc_filled, 4 * T - (3, 2, 0, 0)[g - G_QK])
                if g == G_OUT1 and kt == 0:
                    act.wait_ge(w_lo, split_count(G_OUT0, KT - 1))
                if g == G_OUT1:
                    act.wait_ge(raw_out_loaded[(kt // 2) % 2], 64 + 32 * (kt // 4))
                else:
                    act.wait_ge(raw_loaded[kt // 2], 32 * (g + 1) + (32 if g == G_OUT0 and kt < HALF else 0))
                nc.scalar.activation(dst[:, 0], raw, ACT.Copy, scale=gain).then_inc(w_hi, 1)

        def split_lo(dve, g, kts):
            for kt in kts:
                raw, dst, gain = split_views(g, kt)
                dve.wait_ge(w_hi, split_count(g, kt))
                nc.vector.scalar_tensor_tensor(out=dst[:, 1], in0=raw, scalar=gain, in1=dst[:, 0].bitcast(F32),
                                               op0=ALU.mult, op1=ALU.subtract).then_inc(w_lo, 1)

        def gain_r():
            nc.vector.wait_ge(raw_r_loaded, 16)
            nc.vector.tensor_tensor(stage_r, stage_r, gain_col[:, :].unsqueeze(2).to_broadcast((P, KT, GR)),
                                    ALU.mult).then_inc(r_gained, 1)

        def split_r_hi():
            nc.scalar.wait_ge(r_gained, 1)
            nc.scalar.activation(w_kv[:, 0, :, 2 * AKW:], stage_r, ACT.Copy).then_inc(w_r_hi, 1)

        def split_r_lo():
            nc.vector.wait_ge(w_r_hi, 1)
            nc.vector.tensor_tensor(w_kv[:, 1, :, 2 * AKW:], stage_r, w_kv[:, 0, :, 2 * AKW:].bitcast(F32),
                                    ALU.subtract).then_inc(w_r_lo, 1)

        def ht_bytes(slot):
            return ht[:, slot].rearrange("p s k c -> p (s k c)").bitcast(F32)

        acc = [bank(f"acc{i}") for i in range(2)]
        tp = [bank(f"tp{i}") for i in range(3)]
        sc = [bank(f"sc{i}") for i in range(2)]
        oa = bank("oa")

        with ExitStack() as pa:
            def sba(name, shape, dt=F32):
                return pa.enter_context(nc.sbuf_tensor(name, shape, dt))

            w_kv = sba("w_kv", [P, 2, KT, 2 * AKW + GR], F32R)
            raw_w = sba("raw_w", [P, HALF, 4, 2 * AKW])
            probs = sba("probs", [P, AH, 2 * P])
            probs_t = sba("probs_t", [P, AH, 2, P])
            bias = sba("bias", [P, AH, 3 * P])
            q_s = sba("q_s", [P, AW])
            q2t = sba("q2t", [P, AH, P], F32R)
            k_s = sba("k_s", [P, AKV, 2, AD])
            k2t = sba("k2t", [P, 2, 2, AKV, P], F32R)
            va = sba("va", [P, 2, AKV, AD])
            gate_a = sba("gate_a", [P, 2, AW])
            gate_s = sba("gate_s", [P, AG, AKV, AD])
            gate_t = sba("gate_t", [P, AW])
            gate_g = sba("gate_g", [P, 2, GW])
            mixa = sba("mixa", [P, 2, AW])
            line = mixa[0:AH, 0, 0:3 * P]
            zline = mixa[0:AH, 1, 0:P]
            acc_filled = sem("acc_filled")
            acc_drained = [sem(f"acc_drained{i}") for i in range(2)]
            tp_filled = sem("tp_filled")
            tp_drained = [sem(f"tp_drained{i}") for i in range(3)]
            sc_filled = sem("sc_filled")
            sc_drained = [sem(f"sc_drained{i}") for i in range(2)]
            oa_filled = sem("oa_filled")
            q_hi = sem("q_hi")
            k_hi = sem("k_hi")
            nmx_ready = sem("nmx_ready")
            sinkd_ready = sem("sinkd_ready")
            exp_ready = sem("exp_ready")
            esink_ready = sem("esink_ready")
            den_ready = sem("den_ready")
            rden_ready = sem("rden_ready")
            e_ready = sem("e_ready")
            e1_ready = sem("e1_ready")
            rec_ready = sem("rec_ready")
            gate_ready = sem("gate_ready")
            gate_scaled = sem("gate_scaled")
            mixa_ready = sem("mixa_ready")
            mixa_stored = sem("mixa_stored")
            gate_stored = sem("gate_stored")

            runs = bucket_runs()

            def q_views(odd):
                rows = slice(AD * odd, AD * odd + AD)
                return rows, slice(odd, AH, 2), tp[a_bank(0)][rows, :].rearrange("p (c i) -> p c i", i=P)

            def a_data(eng, t, k):
                eng.wait_ge(tp_drained[a_bank(k)], a_prior(t, k) + 1)

        with ExitStack() as pb:
            def sbb(name, shape, dt=F32):
                return pb.enter_context(nc.sbuf_tensor(name, shape, dt))

            w_out1 = sbb("w_out1", [P, 2, KT, NW], F32R)
            junk_y = sbb("junk_y", [P, D], BF16)
            yb = sbb("yb", [P, 2, D])
            mix = sbb("mix", [P, D])
            mix_t = sbb("mix_t", [P, 2, KT, P], F32R)
            gain_row = sbb("gain_row", [P, D])
            scan_mask = sbb("scan_mask", [P, 2 * P])
            qk = sbb("qk", [P, 2 * GKW])
            vb = sbb("vb", [P, GW])
            l_b = sbb("l_b", [P, 2 * P])
            ls_b = sbb("ls_b", [P, 2 * P])
            b_b = sbb("b_b", [P, 2, 2, GC])
            bl = sbb("bl", [P, 2, 2, 2])
            e_up = sbb("e_up", [P, 2, P])
            e_dn = sbb("e_dn", [P, 2, P])
            q_dec = sbb("q_dec", [P, 2, P])
            k_dec = sbb("k_dec", [P, 2, P])
            k_tok = sbb("k_tok", [P, 2, P])
            a_t = sbb("a_t", [P, 2, 2, P])
            state = sbb("state", [P, 2, GV])
            state_x = sbb("state_x", [P, 2, GV])
            junk_g = sbb("junk_g", [P, GH, GV], BF16)
            fsum = sbb("fsum", [P, 2])
            fexp = sbb("fexp", [P, 2])
            ss4 = sbb("ss4", [P, GH])
            ms4 = sbb("ms4", [P, GH])
            rs4 = sbb("rs4", [P, GH])
            ssy = sbb("ssy", [P, 2])
            msy = sbb("msy", [P, 2])
            rsy = sbb("rsy", [P, 2])
            rb = tp[2]
            at = sc
            ob = oa
            o_b = [ob[:, 0:2 * GV].rearrange("p (j v) -> p j v", v=GV),
                   at[1][:, 256:512].rearrange("p (j v) -> p j v", v=GV)]
            mix_g = mix[:, AW:D].rearrange("p (j o v) -> p o j v", o=2, v=GV)
            u_b = at[0][:, 256:512].rearrange("p (j v) -> p j v", v=GV)

            b_acc_filled = sem("b_acc_filled")
            b_acc_drained = [sem(f"b_acc_drained{i}") for i in range(2)]
            b_tp_filled = sem("b_tp_filled")
            b_tp_drained = [sem(f"b_tp_drained{i}") for i in range(2)]
            r_filled = sem("r_filled")
            r_moved = sem("r_moved")
            rt_copied = sem("rt_copied")
            l_ready = sem("l_ready")
            ls_ready = sem("ls_ready")
            b_scanned = sem("b_scanned")
            bl_ready = sem("bl_ready")
            b_mid = sem("b_mid")
            fsum_ready = sem("fsum_ready")
            fexp_ready = sem("fexp_ready")
            decay_ready = sem("decay_ready")
            at_filled = sem("at_filled")
            at_copied = sem("at_copied")
            at_masked = sem("at_masked")
            u_filled = sem("u_filled")
            x_state = sem("x_state")
            state_ready = sem("state_ready")
            o_filled = sem("o_filled")
            ss4_ready = sem("ss4_ready")
            ms4_ready = sem("ms4_ready")
            rs4_ready = sem("rs4_ready")
            mixg_scaled = sem("mixg_scaled")
            mix_ready = sem("mix_ready")
            mix_hi = sem("mix_hi")
            mix_lo = sem("mix_lo")
            mix_loaded = sem("mix_loaded")
            y_loaded = [sem(f"y_loaded{i}") for i in range(2)]
            ssy_ready = sem("ssy_ready")
            msy_ready = sem("msy_ready")
            rsy_ready = sem("rsy_ready")
            y_scaled = sem("y_scaled")
            out_stored = [sem(f"out_stored{i}") for i in range(2)]
            gain_loaded_b = sem("gain_loaded_b")
            b_set = sem("b_set")

            def pass_a_done(eng):
                eng.wait_ge(oa_filled, T)

            def b_data(eng, t, k):
                eng.wait_ge(b_tp_drained[k % 2], b_prior(t, k) + 1)

            def acc_data(eng, t, g):
                eng.wait_ge(b_acc_drained[g % 2], acc_prior(t, g) + 1)

        w_home = (w_block[0], w_block[1], w_kv, w_block[2], w_block[0], w_block[1], w_block[2], w_out1)

        with nc.Block() as block:
            @block.sync
            def _(sp):
                sp.dma_start(xb[:, 0, :], x_t[0]).then_inc(x_loaded[0], 16)
                sp.dma_start(gain_col[:], norm_gain.rearrange("l (k p) -> (l p) k", p=P),
                             allow_slow_non_contiguous=True).then_inc(gain_loaded, 16)
                for i in range(HALF):
                    load_raw(sp, G_ZA, i)
                sp.dma_start(xb[:, 1, :], x_t[1]).then_inc(x_loaded[1], 16)
                sp.dma_start(rel_t[:], rel_bias.rearrange("b h -> h b"),
                             allow_slow_non_contiguous=True).then_inc(const_loaded, 16)
                sp.dma_start(sink[:], sinks[0].partition_broadcast(P)).then_inc(const_loaded, 16)
                sp.dma_start(gla_gain_col[:], gla_norm_gain.rearrange("l v -> v l"),
                             allow_slow_non_contiguous=True).then_inc(const_loaded, 16)
                sp.dma_start(w_up[0:GR, :], w_gate_up[0]).then_inc(const_loaded, 16)
                sp.dma_start(w_up[GR:, :], b_gate).then_inc(const_loaded, 16)
                for g in (G_ZG, G_KV, G_Q):
                    if g == G_KV:
                        sp.dma_start(stage_r, w_in_k[:, :, C_R:N_IN]).then_inc(raw_r_loaded, 16)
                    for i in range(HALF):
                        load_raw(sp, g, i)
                sp.wait_ge(tp_filled, 2)
                sp.dma_start(xb[:, 0, :], x_t[2]).then_inc(x_loaded[0], 16)
                sp.wait_ge(line_set, 2 + len(runs))
                sp.dma_start(line_dram.ap(), line.unsqueeze(1).to_broadcast((AH, P, 3 * P))).then_inc(line_stored, 16)
                sp.wait_ge(line_stored, 16)
                for h in range(AH):
                    sp.dma_start(bias[:, h, 0:2 * P],
                                 bass.AP(line_dram, h * P * 3 * P + P - 1, [[3 * P - 1, P], [1, 2 * P]]))\
                      .then_inc(bias_loaded, 16)
                for i in range(HALF):
                    load_raw(sp, G_QK, i)

                def step(t, p, index):
                    if not is_t(t, 0):
                        settle(sp)
                        a_data(sp, t - 1, 7)
                        sp.dma_start(ht_dram[t], ht_bytes(p)).then_inc(ht_stored[p], 16)
                    settle(sp)
                    sp.wait_ge(gate_ready, 2 * t + 2)
                    sp.dma_start(mix_dram[t, :, AW:D], gate_g[:, p, :]).then_inc(gate_stored, 16)
                    if not (isinstance(t, int) and t == 0):
                        settle(sp)
                        sp.wait_ge(mixa_ready, t)
                        sp.dma_start(mix_dram[t - 1, :, 0:AW], mixa[:, 1 - p, :]).then_inc(mixa_stored, 16)
                    if not (isinstance(t, int) and t > T - 3):
                        settle(sp)
                        sp.wait_ge(tp_filled, a_filled(t, 7))
                        sp.dma_start(xb[:, 1 - p, :], x_t[index]).then_inc(x_loaded[1 - p], 16)

                step(0, 0, 3)
                step(1, 1, 4)
                with sp.Fori(2, T - 4, 2) as t:
                    step(t, 0, t + 3)
                    step(t + 1, 1, t + 4)
                for t in range(T - 4, T):
                    if t == T - 1:
                        for i in range(HALF):
                            load_raw(sp, G_V, i)
                    step(t, t % 2, (t + 3) % T)
                sp.wait_ge(ht_stored[0], 8 * T - 16)
                sp.wait_ge(ht_stored[1], 8 * T)
                sp.wait_ge(acc_filled, 4 * T)
                sp.dma_start(ht_bytes(1), ht_dram[1]).then_inc(ht_loaded[1], 16)
                for i in range(HALF):
                    load_raw(sp, G_OUT0, i)
                for i in range(2):
                    load_raw(sp, G_OUT1, i)
                sp.wait_ge(mixa_ready, T)
                sp.dma_start(mix_dram[T - 1, :, 0:AW], mixa[:, 1, :]).then_inc(mixa_stored, 16)

                sp.wait_ge(oa_filled, T)
                sp.dma_start(yb[:, 0, :], x_t[0]).then_inc(y_loaded[0], 16)
                sp.dma_start(gain_row[:], final_norm_gain.partition_broadcast(P))\
                  .then_inc(gain_loaded_b, 16)
                sp.wait_ge(mixa_stored, 16 * T)
                sp.wait_ge(gate_stored, 16 * T)
                sp.dma_start(mix[:], mix_dram[0]).then_inc(mix_loaded, 16)

                def step(t, p):
                    if not (isinstance(t, int) and t in (0, T - 1, T)):
                        settle(sp)
                        sp.wait_ge(b_acc_filled, acc_use(t - 1, 1) + 1)
                        sp.dma_start(ht_bytes(1 - p), ht_dram[t + 1]).then_inc(ht_loaded[1 - p], 16)
                    if not (isinstance(t, int) and t < 2):
                        settle(sp)
                        sp.wait_ge(y_scaled, t - 1)
                        sp.dma_start(out_t[t - 2], yb[:, p, :]).then_inc(out_stored[p], 16)
                    if is_t(t, T):
                        return
                    if not is_t(t, 0):
                        settle(sp)
                        sp.wait_ge(b_tp_filled, b_filled(t, 1))
                        sp.dma_start(mix[:], mix_dram[t]).then_inc(mix_loaded, 16)
                        if not is_t(t, 1):
                            settle(sp)
                            sp.wait_ge(out_stored[p], 8 * t if p == 0 else 8 * t - 8)
                        sp.dma_start(yb[:, p, :], x_t[t]).then_inc(y_loaded[p], 16)

                step(0, 0)
                for i in range(2, HALF):
                    load_raw(sp, G_OUT1, i)
                step(1, 1)
                with sp.Fori(2, T - 2, 2) as t:
                    step(t, 0)
                    step(t + 1, 1)
                for t in range(T - 2, T + 1):
                    step(t, t % 2)
                settle(sp)
                sp.wait_ge(y_scaled, T)
                sp.dma_start(out_t[T - 1], yb[:, (T - 1) % 2, :]).then_inc(out_stored[(T - 1) % 2], 16)
                for p in range(2):
                    sp.wait_ge(out_stored[p], 8 * T)

            @block.gpsimd
            def _(pool):
                nc.gpsimd.memset(half[:], -0.5).then_inc(const_set, 1)
                nc.gpsimd.memset(ident[:], 0.0).then_inc(ident_set, 1)
                pool.wait_ge(ident_set, 1)
                nc.gpsimd.affine_select(out=ident[:], in_=ident[:], compare_op=ALU.not_equal,
                                        fill=1.0, base=0, pattern=[[-1, P]],
                                        channel_multiplier=1).then_inc(ident_set, 1)
                nc.gpsimd.memset(r_t[:], 1.0).then_inc(const_set, 1)
                rstd_x(pool, 0, 0)
                pool.wait_ge(const_loaded, 80)
                pool.wait_ge(line_set, 2)
                for a, b, k in runs:
                    nc.gpsimd.tensor_scalar(line[:, a:b], zline[:, 0:b - a], rel_t[:, k:k + 1], None,
                                            ALU.add).then_inc(line_set, 1)

                def add_one(t, j):
                    pool.wait_ge(e_ready, 2 * t + (j + 1))
                    hold(pool)
                    nc.gpsimd.tensor_scalar(ez[:, j, :], ez[:, j, :], 1.0, None, ALU.add)\
                        .then_inc(e1_ready, 1)

                def step(t, p):
                    first = isinstance(t, int) and t == 0
                    second = is_t(t, 1)
                    tail = isinstance(t, int) and t == T
                    if not tail:
                        if not second:
                            rstd_x(pool, t + 1, 1 - p)
                        add_one(t, 0)
                        if first:
                            add_one(t, 1)
                            rstd_x(pool, 2, 0)
                        if is_t(t, 1):
                            pool.wait_ge(bias_loaded, 16 * AH)
                            nc.gpsimd.tensor_copy(bias[:, :, 2 * P:3 * P], bias[:, :, 0:P])\
                                .then_inc(bias_widened, 1)
                        pool.wait_ge(rec_ready, 4 * t + 2)
                        pool.wait_ge(acc_drained[0], 2 * t + 1)
                        nc.gpsimd.tensor_tensor(gate_a[:, p, :], ez[:, 2, :], ez[:, 0, :], ALU.mult)\
                            .then_inc(gate_ready, 1)
                        if not first:
                            add_one(t, 1)
                    if not first:
                        pool.wait_ge(rden_ready, t)
                        if tail:
                            pool.wait_ge(gate_ready, 2 * t - 1)
                        if not second:
                            pool.wait_ge(tp_filled, a_filled(t - 1, 5))
                        nc.gpsimd.tensor_tensor(
                            gate_s[:, :, :, :].rearrange("p i g d -> p g i d"),
                            gate_a[:, 1 - p, :].rearrange("p (g i d) -> p g i d", g=AKV, d=AD),
                            rden[:, :].rearrange("p (g i) -> p g i", g=AKV).unsqueeze(3)
                            .to_broadcast((P, AKV, AG, AD)), ALU.mult).then_inc(gate_scaled, 1)
                    if not tail:
                        pool.wait_ge(rec_ready, 4 * t + 4)
                        pool.wait_ge(acc_drained[1], 2 * t + 1)
                        if not (isinstance(t, int) and t < 2):
                            pool.wait_ge(gate_stored, 16 * t - 16)
                        nc.gpsimd.tensor_tensor(gate_g[:, p, :], ez[:, 3, :], ez[:, 1, :], ALU.mult)\
                            .then_inc(gate_ready, 1)

                steps(pool, step)

                pass_a_done(pool)
                pool.wait_ge(gate_scaled, T)
                nc.gpsimd.memset(state_x[:], 0.0).then_inc(b_set, 1)
                nc.gpsimd.memset(bl[:], 0.0).then_inc(b_set, 1)
                nc.gpsimd.memset(scan_mask[:], 1.0).then_inc(b_set, 1)
                pool.wait_ge(b_set, 3)
                nc.gpsimd.memset(scan_mask[:].rearrange("p (c j) -> p c j", j=GC)[:, :, 0:1], 0.0)\
                    .then_inc(b_set, 1)

                def step(t, p):
                    if not (isinstance(t, int) and t in (0, T - 1, T)):
                        pool.wait_ge(rt_copied, t)
                        hold(pool)
                        nc.gpsimd.tensor_copy(r_in[:, 1 - p, :], r_all[:, t + 1, :]).then_inc(r_moved, 1)
                    if not is_t(t, 0):
                        pool.wait_ge(at_copied, t)
                        hold(pool)
                        nc.gpsimd.affine_select(
                            out=a_t[:], in_=a_t[:], compare_op=ALU.is_ge, fill=0.0, base=0,
                            pattern=[[0, 2], [0, 2], [1, P]], channel_multiplier=-1).then_inc(at_masked, 1)
                    if not (isinstance(t, int) and t < 2):
                        scale_y(t, p)
                    if not is_t(t, 0):
                        pool.wait_ge(ss4_ready, 4 * t)
                        hold(pool)
                        nc.gpsimd.tensor_scalar(ms4[:], ss4[:], 1.0 / GV, EPS, ALU.mult, ALU.add)\
                            .then_inc(ms4_ready, 1)
                        pool.wait_ge(ms4_ready, t)
                        nc.gpsimd.tensor_tensor(rs4[:], ms4[:], half[:, 0:GH], ALU.pow)\
                            .then_inc(rs4_ready, 1)
                        pool.wait_ge(rs4_ready, t)
                        pool.wait_ge(mix_loaded, 16 * t)
                        g = mix[:, AW:D].rearrange("p (h v) -> p h v", v=GV)
                        nc.gpsimd.tensor_tensor(g, g, rs4[:, :].unsqueeze(2).to_broadcast((P, GH, GV)),
                                                ALU.mult).then_inc(mixg_scaled, 1)

                def scale_y(t, p):
                    pool.wait_ge(ssy_ready, t - 1)
                    hold(pool)
                    nc.gpsimd.tensor_scalar(msy[:, p:p + 1], ssy[:, p:p + 1], 1.0 / D, EPS,
                                            ALU.mult, ALU.add).then_inc(msy_ready, 1)
                    pool.wait_ge(msy_ready, t - 1)
                    nc.gpsimd.tensor_tensor(rsy[:, p:p + 1], msy[:, p:p + 1], half[:, 0:1], ALU.pow)\
                        .then_inc(rsy_ready, 1)

                steps(pool, step)
                scale_y(T + 1, 1)

            @block.scalar
            def _(act):
                nc.scalar.preload_act_table_set("natural_log_exp_and_others")
                square_x(act, 0, 0, 16)
                act.wait_ge(gain_loaded, 16)

                def h_part_hi(t, k, slot):
                    if k == 0 and not (isinstance(t, int) and t < 2):
                        act.wait_ge(ht_stored[slot], 8 * t - (0 if slot else 8))
                    act.wait_ge(tp_filled, a_filled(t, 6 + k))
                    nc.scalar.activation(ht[:, slot, 0, HALF * k:HALF * k + HALF, :],
                                         tp[a_bank(6 + k)][:, :].rearrange("p (k c) -> p k c", c=P),
                                         ACT.Copy).then_inc(h_hi, 1)

                split_hi(act, G_ZA, range(2))
                for j in range(2):
                    act.wait_ge(tp_filled, j + 1)
                    nc.scalar.activation(ht[:, 0, 0, HALF * j:HALF * j + HALF, :],
                                         tp[j][:, :].rearrange("p (k c) -> p k c", c=P),
                                         ACT.Copy).then_inc(h_hi, 1)
                split_hi(act, G_ZA, range(2, KT))
                split_hi(act, G_ZG, range(KT))

                def r_out(t):
                    act.wait_ge(r_filled, 2 * t + 1)
                    nc.scalar.activation(r_t[0:GR, :], rb[0:GR, 0:P], ACT.Copy).then_inc(rt_copied, 1)

                def step(t, p):
                    first = isinstance(t, int) and t == 0
                    second = isinstance(t, int) and t == 1
                    tail = isinstance(t, int) and t == T
                    cols = P if second else 2 * P
                    if not tail:
                        square_x(act, t + 1, 1 - p, 8 * t + (16 if p == 0 else 24))
                    if not first:
                        act.wait_ge(tp_filled, a_filled(t, 0))
                        for odd in range(2):
                            rows, heads, src = q_views(odd)
                            nc.scalar.activation(q2t[rows, heads, :], src, ACT.Copy).then_inc(q_hi, 1)

                    def exp_z(j):
                        act.wait_ge(acc_filled, 4 * t + (j + 1))
                        if not first:
                            act.wait_ge(gate_ready, 2 * t + (j - 1))
                        nc.scalar.activation(ez[:, j, :], acc[j][:, :], ACT.Exp, scale=-1.0)\
                            .then_inc(e_ready, 1)
                        nc.scalar.activation(ez[:, 2 + j, :], acc[j][:, :], ACT.Copy)\
                            .then_inc(acc_drained[j], 1)

                    def exps(h0):
                        act.wait_ge(nmx_ready, 2 * t + (h0 // 4 - 1))
                        for h in range(h0, h0 + 4):
                            nc.scalar.activation(probs[:, h, 0:cols], probs[:, h, 0:cols], ACT.Exp,
                                                 bias=nmx[:, h:h + 1],
                                                 accum_out=psum_row[:, h:h + 1]).then_inc(exp_ready, 1)

                    def probs_t_out(j):
                        act.wait_ge(tp_filled, a_filled(t, 1 + j))
                        b = a_bank(1 + j)
                        src = tp[b][:, :].rearrange("p (h s c) -> p h s c", h=2, s=2)
                        nc.scalar.activation(probs_t[:, 2 * j:2 * j + 2, 0:cols // P, :], src[:, :, 0:cols // P, :],
                                             ACT.Copy).then_inc(tp_drained[b], 1)

                    last = isinstance(t, int) and t == T - 1
                    if not tail:
                        exp_z(0)
                    if first:
                        split_r_hi()
                        split_hi(act, G_KV, range(KT))
                    if last:
                        split_hi(act, G_QK, range(2))
                    if tail:
                        split_hi(act, G_V, range(4, 8))
                    if not first:
                        exps(0)
                    if last:
                        split_hi(act, G_QK, range(2, 4))
                    if not first:
                        exps(4)
                        act.wait_ge(sinkd_ready, t)
                        nc.scalar.activation(esink[:], sinkd[:], ACT.Exp).then_inc(esink_ready, 1)
                        probs_t_out(0)
                    if not tail:
                        exp_z(1)
                    if first:
                        split_hi(act, G_Q, range(KT))
                    if not first:
                        probs_t_out(2)
                    if last:
                        split_hi(act, G_QK, range(4, 8))
                    if tail:
                        r_out(0)
                    if not first:
                        if not second:
                            act.wait_ge(mixa_ready, t - 1)
                        act.wait_ge(tp_filled, a_filled(t, 5))
                        nc.scalar.activation(gate_t[:], tp[a_bank(5)][:, :], ACT.Copy)\
                            .then_inc(tp_drained[a_bank(5)], 1)
                    if not tail:
                        h_part_hi(t, 0, 1 - p)
                        h_part_hi(t, 1, 1 - p)
                        act.wait_ge(tp_filled, a_filled(t, 8))
                        nc.scalar.activation(k2t[:, 0, p, :, :], tp[a_bank(8)][:, 0:AKV * P].rearrange(
                            "p (h c) -> p h c", h=AKV), ACT.Copy).then_inc(k_hi, 1)
                        act.wait_ge(acc_filled, 4 * t + 4)
                        if not first:
                            act.wait_ge(tp_filled, a_filled(t, 0))
                        nc.scalar.activation(q_s[:], acc[1][:, :], ACT.Copy, scale=AD ** -0.5)\
                            .then_inc(acc_drained[1], 1)
                    if last:
                        split_hi(act, G_V, range(4))

                steps(act, step)

                pass_a_done(act)

                def hi_part(t, k, dst, counter):
                    act.wait_ge(b_tp_filled, b_filled(t, k))
                    nc.scalar.activation(dst, tp[k % 2][:, :].rearrange("p (k c) -> p k c", c=P),
                                         ACT.Copy).then_inc(counter, 1)

                def mix_hi_part(t):
                    act.wait_ge(mix_loaded, 16 * t)
                    if not is_t(t, 1):
                        act.wait_ge(b_acc_filled, acc_use(t - 1, 3) + 1)
                    nc.scalar.activation(mix_t[:, 0, 0:HALF, :], mix[:, 0:AW].rearrange(
                        "p (k c) -> p k c", c=P), ACT.Copy).then_inc(mix_hi, 1)

                def square_y(t, p):
                    act.wait_ge(b_acc_drained[1], acc_prior(t - 1, 3) + 1)
                    nc.scalar.activation(junk_y[:], yb[:, p, :], ACT.Square,
                                         accum_out=ssy[:, p:p + 1]).then_inc(ssy_ready, 1)

                def step(t, p):
                    first, tail = is_t(t, 0), is_t(t, T)
                    if not (isinstance(t, int) and (t < 2 or t == T)):
                        square_y(t, p)
                    if not (first or tail):
                        r_out(t)
                    if not first:
                        act.wait_ge(at_filled, t)
                        nc.scalar.activation(a_t[:, 0, :, :], at[0][:, 0:2 * P].rearrange(
                            "p (j c) -> p j c", c=P), ACT.Copy)
                        nc.scalar.activation(a_t[:, 1, :, :], at[1][:, 0:2 * P].rearrange(
                            "p (j c) -> p j c", c=P), ACT.Copy).then_inc(at_copied, 1)
                        mix_hi_part(t)
                    if tail:
                        square_y(t, p)
                    if is_t(t, 1):
                        split_hi(act, G_OUT0, range(KT))
                    if not tail:
                        act.wait_ge(b_acc_filled, acc_use(t, 0) + 1)
                        nc.scalar.activation(qk[:, 0:GKW], acc[0][:, 0:GKW], ACT.Copy,
                                             scale=GK ** -0.5)
                        nc.scalar.activation(qk[:, GKW:], acc[0][:, GKW:], ACT.Copy)\
                            .then_inc(b_acc_drained[0], 1)
                        act.wait_ge(r_filled, 2 * t + 2)
                        if not first:
                            act.wait_ge(ls_ready, t)
                        y = rb[:, 256:512]
                        nc.scalar.activation(l_b[:], y, ACT.Abs).then_inc(l_ready, 1)
                        act.wait_ge(l_ready, 3 * t + 1)
                        nc.scalar.activation(l_b[:], l_b[:], ACT.Exp, scale=-1.0).then_inc(l_ready, 1)
                        act.wait_ge(l_ready, 3 * t + 2)
                        nc.scalar.activation(l_b[:], l_b[:], ACT.Ln, bias=1.0).then_inc(l_ready, 1)
                    if not first:
                        act.wait_ge(o_filled, t)
                        if not is_t(t, 1):
                            act.wait_ge(ms4_ready, t - 1)
                        for h in range(GH):
                            nc.scalar.activation(junk_g[:, h, :], o_b[h % 2][:, h // 2, :], ACT.Square,
                                                 accum_out=ss4[:, h:h + 1]).then_inc(ss4_ready, 1)
                    if not tail:
                        act.wait_ge(fsum_ready, t + 1)
                        nc.scalar.activation(fexp[:], fsum[:], ACT.Exp, scale=1.0 / GATE_NORM)\
                            .then_inc(fexp_ready, 1)
                    if not tail:
                        act.wait_ge(b_mid, t + 1)
                        bb = b_b[:, :, :, :].rearrange("p j c i -> p j (c i)")
                        nc.scalar.activation(e_up[:], bb, ACT.Exp, scale=1.0 / GATE_NORM)
                        nc.scalar.activation(e_dn[:], bb, ACT.Exp, scale=-1.0 / GATE_NORM)\
                            .then_inc(decay_ready, 1)
                        if is_t(t, 1):
                            split_hi(act, G_OUT1, range(HALF))
                        act.wait_ge(b_acc_filled, acc_use(t, 1) + 1)
                        nc.scalar.activation(vb[:], acc[1][:, :], ACT.Copy).then_inc(b_acc_drained[1], 1)
                    if not first:
                        hi_part(t, 1, mix_t[:, 0, HALF:KT, :], mix_hi)
                    if is_t(t, 1):
                        split_hi(act, G_OUT1, range(HALF, KT))
                    if not tail:
                        act.wait_ge(b_tp_filled, b_filled(t, 3))
                        nc.scalar.activation(k_tok[:], tp[1][:, 0:2 * P].rearrange(
                            "p (j c) -> p j c", c=P), ACT.Copy).then_inc(b_tp_drained[1], 1)

                steps(act, step)
                square_y(T + 1, 1)

            @block.vector
            def _(dve):
                nc.vector.memset(line, NEG).then_inc(line_set, 1)
                nc.vector.memset(zline, 0.0).then_inc(line_set, 1)
                scale_x(dve, 0, 0)
                split_lo(dve, G_ZA, range(2))
                for j in range(2):
                    dve.wait_ge(h_hi, j + 1)
                    nc.vector.tensor_tensor(ht[:, 0, 1, HALF * j:HALF * j + HALF, :],
                                            tp[j][:, :].rearrange("p (k c) -> p k c", c=P),
                                            ht[:, 0, 0, HALF * j:HALF * j + HALF, :].bitcast(F32),
                                            ALU.subtract).then_inc(tp_drained[j], 1)
                split_lo(dve, G_ZA, range(2, KT))
                split_lo(dve, G_ZG, range(KT))
                gain_r()

                def step(t, p):
                    first = isinstance(t, int) and t == 0
                    second = isinstance(t, int) and t == 1
                    tail = isinstance(t, int) and t == T
                    cols = P if second else 2 * P

                    def bias_max(h0):
                        for h in range(h0, h0 + 4):
                            dve.wait_ge(sc_filled, 4 * t + (h // 2 - 3))
                            hold(dve)
                            b = (h // 2) % 2
                            src = sc[b][:, (h % 2) * 2 * P:(h % 2) * 2 * P + cols]
                            last = nc.vector.tensor_tensor_reduce(
                                probs[:, h, 0:cols], src, bias[:, h, p * P:p * P + cols], 1.0, sink[:, h:h + 1],
                                ALU.add, ALU.max, mx[:, h:h + 1])
                            if h % 2:
                                last.then_inc(sc_drained[b], 1)
                        dve.wait_ge(sc_drained[0], 2 * t + (h0 // 4 - 1))
                        dve.wait_ge(sc_drained[1], 2 * t + (h0 // 4 - 1))
                        nc.vector.tensor_scalar(nmx[:, h0:h0 + 4], mx[:, h0:h0 + 4], -1.0, None,
                                                ALU.mult).then_inc(nmx_ready, 1)

                    def recip(j, c, tile=t):
                        dve.wait_ge(e1_ready, 2 * tile + (j + 1))
                        nc.vector.reciprocal(ez[:, j, 256 * c:256 * c + 256],
                                             ez[:, j, 256 * c:256 * c + 256]).then_inc(rec_ready, 1)

                    def probs_t_out(j):
                        dve.wait_ge(tp_filled, a_filled(t, 1 + j))
                        b = a_bank(1 + j)
                        src = tp[b][:, :].rearrange("p (h s c) -> p h s c", h=2, s=2)
                        nc.vector.tensor_copy(probs_t[:, 2 * j:2 * j + 2, 0:cols // P, :],
                                              src[:, :, 0:cols // P, :]).then_inc(tp_drained[b], 1)

                    if not tail:
                        scale_x(dve, t + 1, 1 - p)
                    last_tile = isinstance(t, int) and t == T - 1
                    if first:
                        split_r_lo()
                        split_lo(dve, G_KV, range(KT))
                        split_lo(dve, G_Q, range(KT))
                    if not first:
                        dve.wait_ge(q_hi, 2 * t)
                        for odd in range(2):
                            rows, heads, src = q_views(odd)
                            other = slice(AD - AD * odd, 2 * AD - AD * odd)
                            last = nc.vector.tensor_tensor(q2t[other, heads, :], src,
                                                           q2t[rows, heads, :].bitcast(F32), ALU.subtract)
                        last.then_inc(tp_drained[a_bank(0)], 1)
                        if second:
                            recip(1, 0, 0)
                            recip(1, 1, 0)
                        if tail:
                            split_lo(dve, G_V, range(4, 6))
                        if second:
                            dve.wait_ge(bias_loaded, 16 * AH)
                        bias_max(0)
                    if last_tile:
                        split_lo(dve, G_QK, range(2))
                    if tail:
                        split_lo(dve, G_V, range(6, 8))
                    if not (first or tail):
                        recip(0, 0)
                    if not first:
                        bias_max(4)
                        dve.wait_ge(nmx_ready, 2 * t)
                        nc.vector.tensor_tensor(sinkd[:], sink[:], nmx[:], ALU.add).then_inc(sinkd_ready, 1)
                    if last_tile:
                        split_lo(dve, G_QK, range(2, 4))
                    if not (first or tail):
                        recip(0, 1)
                    if not first:
                        probs_t_out(1)
                        dve.wait_ge(exp_ready, 8 * t)
                        dve.wait_ge(esink_ready, t)
                        nc.vector.tensor_tensor(den[:], psum_row[:], esink[:], ALU.add).then_inc(den_ready, 1)
                        dve.wait_ge(den_ready, t)
                        nc.vector.reciprocal(rden[:], den[:]).then_inc(rden_ready, 1)
                        probs_t_out(3)
                    if last_tile:
                        split_lo(dve, G_QK, range(4, 8))
                    if not tail:
                        if not first:
                            recip(1, 0)
                        dve.wait_ge(acc_filled, 4 * t + 3)
                        if not first:
                            dve.wait_ge(tp_filled, a_filled(t, 0))
                        for c in range(2):
                            nc.vector.tensor_copy(k_s[:, :, c, :], acc[0][:, 0:AKW].rearrange(
                                "p (h d) -> p h d", d=AD))
                        nc.vector.tensor_copy(r_all[:, t, :], acc[0][:, 2 * AKW:2 * AKW + GR])
                        if not first:
                            dve.wait_ge(oa_filled, t)
                        nc.vector.tensor_copy(va[:, p, :, :], acc[0][:, AKW:2 * AKW].rearrange(
                            "p (h d) -> p h d", d=AD)).then_inc(acc_drained[0], 1)
                    if not first:
                        dve.wait_ge(oa_filled, t)
                        a_data(dve, t, 5)
                        if not second:
                            dve.wait_ge(mixa_stored, 16 * t - 16)
                        nc.vector.tensor_tensor(mixa[:, 1 - p, :], oa[:, :], gate_t[:],
                                                ALU.mult).then_inc(mixa_ready, 1)
                    if not tail:
                        for k in range(2):
                            dve.wait_ge(h_hi, 2 * t + (3 + k))
                            nc.vector.tensor_tensor(
                                ht[:, 1 - p, 1, HALF * k:HALF * k + HALF, :],
                                tp[a_bank(6 + k)][:, :].rearrange("p (k c) -> p k c", c=P),
                                ht[:, 1 - p, 0, HALF * k:HALF * k + HALF, :].bitcast(F32),
                                ALU.subtract).then_inc(tp_drained[a_bank(6 + k)], 1)
                        if first:
                            recip(0, 0)
                            recip(0, 1)
                        else:
                            recip(1, 1)
                        dve.wait_ge(k_hi, t + 1)
                        nc.vector.tensor_tensor(k2t[:, 1, p, :, :], tp[a_bank(8)][:, 0:AKV * P].rearrange(
                            "p (h c) -> p h c", h=AKV), k2t[:, 0, p, :, :].bitcast(F32), ALU.subtract)\
                            .then_inc(tp_drained[a_bank(8)], 1)
                    if second:
                        dve.wait_ge(bias_widened, 1)
                    if last_tile:
                        split_lo(dve, G_V, range(4))

                steps(dve, step)

                pass_a_done(dve)
                dve.wait_ge(b_set, 4)

                def lo_part(t, k, dst, hi, counter, count):
                    dve.wait_ge(counter, count)
                    nc.vector.tensor_tensor(dst, tp[k % 2][:, :].rearrange("p (k c) -> p k c", c=P),
                                            hi.bitcast(F32), ALU.subtract).then_inc(b_tp_drained[k % 2], 1)

                def mix_lo_part(t):
                    dve.wait_ge(mix_hi, 2 * t - 1)
                    nc.vector.tensor_tensor(mix_t[:, 1, 0:HALF, :], mix[:, 0:AW].rearrange(
                        "p (k c) -> p k c", c=P), mix_t[:, 0, 0:HALF, :].bitcast(F32), ALU.subtract)\
                        .then_inc(mix_lo, 1)

                def finish(t, p):
                    if is_t(t, 2):
                        dve.wait_ge(gain_loaded_b, 16)
                    dve.wait_ge(rsy_ready, t - 1)
                    nc.vector.scalar_tensor_tensor(out=yb[:, p, :], in0=yb[:, p, :], scalar=rsy[:, p:p + 1],
                                                   in1=gain_row[:], op0=ALU.mult, op1=ALU.mult)\
                        .then_inc(y_scaled, 1)

                def step(t, p):
                    first, tail = is_t(t, 0), is_t(t, T)
                    if tail:
                        mix_lo_part(t)
                    if not (isinstance(t, int) and t < 2):
                        finish(t, p)
                    if not (first or tail):
                        dve.wait_ge(u_filled, t)
                        dve.wait_ge(state_ready, 2 * t)
                        nc.vector.tensor_tensor(state_x[:], u_b, state[:], ALU.add).then_inc(x_state, 1)
                        mix_lo_part(t)
                        if is_t(t, 1):
                            split_lo(dve, G_OUT0, range(KT))
                    if not tail:
                        dve.wait_ge(l_ready, 3 * t + 3)
                        nc.vector.scalar_tensor_tensor(out=ls_b[:], in0=rb[:, 256:512], scalar=0.0,
                                                       in1=l_b[:], op0=ALU.min, op1=ALU.subtract)\
                            .then_inc(ls_ready, 1)
                        dve.wait_ge(ls_ready, t + 1)
                        if not first:
                            dve.wait_ge(decay_ready, t)
                        nc.vector.tensor_tensor_scan(
                            b_b[:].rearrange("p j c i -> p (j c i)"), scan_mask[:], ls_b[:], 0.0,
                            ALU.mult, ALU.add).then_inc(b_scanned, 1)
                        dve.wait_ge(b_scanned, t + 1)
                        nc.vector.tensor_copy(bl[:, p, :, :], b_b[:, :, :, GC - 1]).then_inc(bl_ready, 1)
                        dve.wait_ge(bl_ready, t + 1)
                        nc.vector.tensor_tensor(fsum[:], bl[:, p, :, 0], bl[:, 1 - p, :, 1], ALU.add)\
                            .then_inc(fsum_ready, 1)
                        nc.vector.tensor_tensor(b_b[:, :, 0, :], b_b[:, :, 0, :],
                                                bl[:, p, :, 0:1].to_broadcast((P, 2, GC)),
                                                ALU.subtract).then_inc(b_mid, 1)
                    if not first:
                        dve.wait_ge(o_filled, t)
                    if not tail:
                        dve.wait_ge(fexp_ready, t + 1)
                        if not first:
                            dve.wait_ge(x_state, t)
                        for j in range(2):
                            nc.vector.tensor_scalar(state[:, j, :], state_x[:, j, :], fexp[:, j:j + 1], None,
                                                    ALU.mult).then_inc(state_ready, 1)
                    if not first:
                        dve.wait_ge(mixg_scaled, t)
                        for o in range(2):
                            last = nc.vector.tensor_tensor(mix_g[:, o], o_b[o], mix_g[:, o], ALU.mult)
                        last.then_inc(mix_ready, 1)
                        if is_t(t, 1):
                            split_lo(dve, G_OUT1, range(HALF))
                        lo_part(t, 1, mix_t[:, 1, HALF:KT, :], mix_t[:, 0, HALF:KT, :], mix_hi, 2 * t)
                    if not tail:
                        dve.wait_ge(decay_ready, t + 1)
                        dve.wait_ge(b_tp_filled, b_filled(t, 2))
                        nc.vector.tensor_tensor(q_dec[:], tp[0][:, 0:2 * P].rearrange(
                            "p (j c) -> p j c", c=P), e_up[:], ALU.mult)
                        nc.vector.tensor_tensor(k_dec[:], tp[0][:, 2 * P:4 * P].rearrange(
                            "p (j c) -> p j c", c=P), e_dn[:], ALU.mult).then_inc(b_tp_drained[0], 1)
                    if is_t(t, 1):
                        split_lo(dve, G_OUT1, range(HALF, KT))
                    if not first:
                        for g in range(2):
                            dve.wait_ge(b_acc_filled, acc_use(t, 2 + g) + 1)
                            if g == 0:
                                dve.wait_ge(y_loaded[1 - p], 8 * t + (8 if p else 0))
                            half_y = yb[:, 1 - p, 512 * g:512 * g + 512]
                            nc.vector.tensor_tensor(half_y, acc[g][:, :], half_y, ALU.add)\
                                .then_inc(b_acc_drained[g], 1)

                steps(dve, step)
                finish(T + 1, 1)

            @block.tensor
            def _(pe):
                def h_transposes(t, k, slot, xslot):
                    b = a_bank(6 + k)
                    for c in range(4):
                        kt = HALF * k + c
                        last = nc.tensor.transpose(tp[b][:, c * P:(c + 1) * P],
                                                   xb[:, xslot, kt * P:(kt + 1) * P], ident[:])
                    last.then_inc(tp_filled, 1)

                def project_b(b, g, p, kts, unsplit):
                    for kt in kts:
                        if unsplit:
                            pe.wait_ge(w_lo, split_count(g, kt))
                        for i, (a, w) in enumerate(((0, 0), (0, 1), (1, 0))):
                            last = nc.tensor.matmul(acc[b][:, :], ht[:, p, a, kt, :],
                                                    w_home[g][:, w, kt, :],
                                                    start=(kt == 0 and i == 0), stop=(kt == KT - 1 and i == 2))
                    if KT - 1 in kts:
                        last.then_inc(b_acc_filled, 1)

                def gate_product(t):
                    pe.wait_ge(rt_copied, t + 1)
                    for j in range(2):
                        last = nc.tensor.matmul(rb[:, 256 + j * P:256 + (j + 1) * P],
                                                w_up[:, j * P:(j + 1) * P], r_t[:], start=True, stop=True)
                    last.then_inc(r_filled, 1)

                def transpose_r(t, p):
                    src = r_all[:, t, :] if is_t(t, 0) or is_t(t, 1) else r_in[:, p, :]
                    nc.tensor.transpose(rb[0:GR, 0:P], src, ident[:]).then_inc(r_filled, 1)

                pe.wait_ge(ident_set, 2)
                pe.wait_ge(h_ready, 1)
                for j in range(2):
                    for c in range(4):
                        kt = HALF * j + c
                        last = nc.tensor.transpose(tp[j][:, c * P:(c + 1) * P],
                                                   xb[:, 0, kt * P:(kt + 1) * P], ident[:])
                    last.then_inc(tp_filled, 1)

                def step(t, p):
                    first = isinstance(t, int) and t == 0
                    second = isinstance(t, int) and t == 1
                    tail = isinstance(t, int) and t == T

                    def project(g, halves):
                        b, n = g % 2, G_COLS[g][1] + (GR if g == G_KV else 0)
                        if 0 in halves and not (first and g < 2):
                            pe.wait_ge(acc_drained[b], 2 * t + g // 2)
                        for half_ in halves:
                            for kt in range(HALF * half_, HALF * half_ + HALF):
                                if first:
                                    pe.wait_ge(w_lo, split_count(g, kt))
                                if first and g == G_KV and kt == 0:
                                    pe.wait_ge(w_r_lo, 1)
                                hi, lo = ht[:, p, 0, kt, :], ht[:, p, 1, kt, :]
                                for i, (a, w) in enumerate(((hi, 0), (hi, 1), (lo, 0))):
                                    last = nc.tensor.matmul(acc[b][:, 0:n], a, w_home[g][:, w, kt, :],
                                                            start=(kt == 0 and i == 0),
                                                            stop=(kt == KT - 1 and i == 2))
                        if 1 in halves:
                            last.then_inc(acc_filled, 1)

                    def q_transposes():
                        b = a_bank(0)
                        pe.wait_ge(tp_drained[b], a_prior(t, 0))
                        pe.wait_ge(acc_drained[1], 2 * t)
                        for c in range(4):
                            last = nc.tensor.transpose(tp[b][:, c * P:(c + 1) * P],
                                                       q_s[:, c * P:(c + 1) * P], ident[:])
                        last.then_inc(tp_filled, 1)

                    def scores(h0):
                        if h0 == 0:
                            a_data(pe, t, 0)
                        if h0 == 0:
                            a_data(pe, t - 1, 8)
                        for h in range(h0, h0 + 4):
                            b = (h // 2) % 2
                            if h % 2 == 0 and not (second and h0 == 0):
                                pe.wait_ge(sc_drained[b], 2 * t + (h0 // 4 - 2))
                            slots = 1 if second else 2
                            for w in range(2):
                                last = nc.tensor.matmul(
                                    sc[b][:, (h % 2) * 2 * P:(h % 2) * 2 * P + slots * P],
                                    q2t[:, h, :], k2t[:, w, 0:slots, h // AG, :],
                                    start=(w == 0), stop=(w == 1))
                            if h % 2:
                                last.then_inc(sc_filled, 1)

                    def probs_transposes(j):
                        b = a_bank(1 + j)
                        pe.wait_ge(tp_drained[b], a_prior(t, 1 + j))
                        pe.wait_ge(exp_ready, 8 * t + (2 * j - 6))
                        for h in range(2):
                            for s in range(1 if second else 2):
                                last = nc.tensor.transpose(tp[b][:, (2 * h + s) * P:(2 * h + s + 1) * P],
                                                           probs[:, 2 * j + h, s * P:(s + 1) * P], ident[:])
                        last.then_inc(tp_filled, 1)

                    def attend():
                        if not second:
                            pe.wait_ge(mixa_ready, t - 1)
                        pe.wait_ge(acc_drained[0], 2 * t)
                        for j in range(4):
                            a_data(pe, t, 1 + j)
                        slots = 1 if second else 2
                        for s in range(slots):
                            for g in range(AKV):
                                last = nc.tensor.matmul(oa[AD * g:AD * g + AD, :], va[:, s, g, :],
                                                        probs_t[:, AG * g:AG * g + AG, s, :],
                                                        start=(s == 0), stop=(s == slots - 1))
                        last.then_inc(oa_filled, 1)

                    def gate_transposes():
                        b = a_bank(5)
                        pe.wait_ge(tp_drained[b], a_prior(t, 5))
                        pe.wait_ge(gate_scaled, t)
                        for i in range(AG):
                            last = nc.tensor.transpose(tp[b][:, i * P:(i + 1) * P],
                                                       gate_s[:, i, :, :].rearrange("p g d -> p (g d)"),
                                                       ident[:])
                        last.then_inc(tp_filled, 1)

                    if tail:
                        for k in range(2):
                            a_data(pe, t - 1, 6 + k)
                        pe.wait_ge(acc_drained[0], 2 * T)
                        project_b(0, G_QK, 0, range(HALF), True)
                        q_transposes()
                        project_b(0, G_QK, 0, range(HALF, KT), True)
                        scores(0)
                        project_b(1, G_V, 0, range(HALF), True)
                        scores(4)
                        probs_transposes(0)
                        probs_transposes(1)
                        project_b(1, G_V, 0, range(HALF, KT), True)
                        probs_transposes(2)
                        probs_transposes(3)
                        pe.wait_ge(tp_drained[2], 3 * T)
                        transpose_r(0, 0)
                        attend()
                        gate_product(0)
                        gate_transposes()
                        return
                    if first:
                        pe.wait_ge(tp_drained[0], 1)
                        pe.wait_ge(tp_drained[1], 1)
                    else:
                        for k in range(2):
                            a_data(pe, t - 1, 6 + k)
                    project(G_ZA, (0,))
                    if not first:
                        q_transposes()
                    project(G_ZA, (1,))
                    if not first:
                        scores(0)
                    project(G_ZG, (0,))
                    if not first:
                        scores(4)
                    project(G_ZG, (1,))
                    if not first:
                        probs_transposes(0)
                        probs_transposes(1)
                    project(G_KV, (0,))
                    if not first:
                        probs_transposes(2)
                        probs_transposes(3)
                    project(G_KV, (1,))
                    if not first:
                        attend()
                        gate_transposes()
                    pe.wait_ge(h_ready, t + 2)
                    for k in range(2):
                        pe.wait_ge(tp_drained[a_bank(6 + k)], a_prior(t, 6 + k))
                        h_transposes(t, k, 1 - p, 1 - p)
                    project(G_Q, (0, 1) if first else (0,))
                    pe.wait_ge(tp_drained[a_bank(8)], a_prior(t, 8))
                    pe.wait_ge(acc_drained[0], 2 * t + 2)
                    for h in range(AKV):
                        last = nc.tensor.transpose(tp[a_bank(8)][:, h * P:(h + 1) * P],
                                                   k_s[:, h, :, :].rearrange("p c d -> p (c d)"), ident[:])
                    last.then_inc(tp_filled, 1)
                    if not first:
                        project(G_Q, (1,))

                steps(pe, step)

                def step(t, p):
                    first, second, tail = is_t(t, 0), is_t(t, 1), is_t(t, T)

                    def acc_free(g, at=t):
                        if not (first or (second and acc_prior(t, g) < 1)):
                            pe.wait_ge(b_acc_drained[g % 2], acc_prior(at, g))

                    def output(g, kts, at=t):
                        if 0 in kts:
                            acc_free(2 + g, at)
                        for kt in kts:
                            if second:
                                pe.wait_ge(w_lo, split_count(G_OUT0 + g, kt))
                            for i, (a, w) in enumerate(((0, 0), (0, 1), (1, 0))):
                                last = nc.tensor.matmul(acc[g][:, :], mix_t[:, a, kt, :],
                                                        w_home[G_OUT0 + g][:, w, kt, :],
                                                        start=(kt == 0 and i == 0),
                                                        stop=(kt == KT - 1 and i == 2))
                        if KT - 1 in kts:
                            last.then_inc(b_acc_filled, 1)

                    def tp_free(k):
                        if first:
                            pe.wait_ge(tp_drained[k % 2], 3 * T + 1)
                        else:
                            pe.wait_ge(b_tp_drained[k % 2], b_prior(t, k))

                    if not tail:
                        if not (first or second):
                            pe.wait_ge(ht_loaded[p], 8 * t + (0 if p == 0 else 8))
                        if not (first or second):
                            pe.wait_ge(ls_ready, t)
                            pe.wait_ge(r_moved, t - 1)
                            transpose_r(t, p)
                    if not first:
                        b_data(pe, t - 1, 2)
                        if not second:
                            pe.wait_ge(x_state, t - 1)
                            pe.wait_ge(at_copied, t - 1)
                            pe.wait_ge(mix_ready, t - 1)
                        for o in range(2):
                            rows = slice(GK * o, GK * o + GK)
                            for j in range(2):
                                last = nc.tensor.matmul(at[o][:, j * P:(j + 1) * P], k_dec[rows, j, :],
                                                        q_dec[rows, j, :], start=True, stop=True)
                        last.then_inc(at_filled, 1)
                    if not (first or second or tail):
                        acc_free(0)
                        project_b(0, G_QK, p, range(HALF), False)
                    if not (first or tail):
                        b_data(pe, t - 1, 3)
                        acc_data(pe, t - 1, 1)
                        pe.wait_ge(at_copied, t)
                        for h in range(GH):
                            rows = slice(GK * (h % 2), GK * (h % 2) + GK)
                            last = nc.tensor.matmul(u_b[rows, h // 2, :], k_tok[:, h // 2, rows],
                                                    vb[:, h * GV:(h + 1) * GV], start=True, stop=True)
                        last.then_inc(u_filled, 1)
                    if tail:
                        acc_data(pe, t - 1, 1)
                    if not (first or tail):
                        project_b(0, G_QK, p, range(HALF, KT), False)
                        gate_product(t)
                    if tail:
                        output(1, range(KT), t - 1)
                    if not first:
                        pe.wait_ge(at_masked, t)
                        pe.wait_ge(state_ready, 2 * t)
                        if second:
                            pe.wait_ge(mixa_ready, T)
                        for h in range(GH):
                            rows = slice(GK * (h % 2), GK * (h % 2) + GK)
                            dst = o_b[h % 2][:, h // 2, :]
                            nc.tensor.matmul(dst, q_dec[rows, h // 2, :], state[rows, h // 2, :],
                                             start=True, stop=False)
                            last = nc.tensor.matmul(dst, a_t[:, h % 2, h // 2, :],
                                                    vb[:, h * GV:(h + 1) * GV], start=False, stop=True)
                        last.then_inc(o_filled, 1)
                        if tail:
                            pe.wait_ge(mix_lo, t)
                            output(0, range(HALF))
                            output(1, range(HALF))
                    if not (first or tail):
                        acc_free(1)
                        project_b(1, G_V, p, range(KT), False)
                    if not first:
                        tp_free(1)
                        pe.wait_ge(mix_ready, t)
                        for c in range(HALF):
                            last = nc.tensor.transpose(tp[1][:, c * P:(c + 1) * P],
                                                       mix[:, AW + c * P:AW + (c + 1) * P], ident[:])
                        last.then_inc(b_tp_filled, 1)
                    if not tail:
                        tp_free(2)
                        acc_data(pe, t, 0)
                        for c in range(4):
                            last = nc.tensor.transpose(tp[0][:, c * P:(c + 1) * P],
                                                       qk[:, c * P:(c + 1) * P], ident[:])
                        last.then_inc(b_tp_filled, 1)
                    if not (first or tail):
                        pe.wait_ge(mix_lo, t)
                        output(0, range(HALF))
                    if not first:
                        b_data(pe, t, 1)
                        output(0, range(HALF, KT))
                    if first:
                        pe.wait_ge(ht_loaded[1], 16)
                        pe.wait_ge(b_acc_drained[0], 1)
                        project_b(0, G_QK, 1, range(HALF), False)
                        pe.wait_ge(ls_ready, 1)
                        transpose_r(1, 1)
                    if not tail:
                        tp_free(3)
                        b_data(pe, t, 2)
                        for j in range(2):
                            last = nc.tensor.transpose(tp[1][:, j * P:(j + 1) * P], k_dec[:, j, :], ident[:])
                        last.then_inc(b_tp_filled, 1)
                    if tail:
                        output(1, range(HALF, KT))
                    elif not (first or is_t(t, T - 1)):
                        output(1, range(KT))

                steps(pe, step)


_INS = ["x", "norm_gain", "w_in", "w_gate_up", "b_gate", "rel_bias", "sinks", "gla_norm_gain", "w_out",
        "final_norm_gain"]


def kernel(**inputs):
    import numpy as _np
    import concourse.bacc as _bacc
    from concourse import mybir as _mybir
    from concourse.bass_utils import run_bass_kernel_spmd as _run

    nc = _bacc.Bacc("TRN2", target_bir_lowering=False, num_devices=1, dynamic_dma_scratch_size=1024)
    arrays, args = {}, []
    for name in _INS:
        a = _np.ascontiguousarray(inputs[name])
        arrays[f"in_{name}_dram"] = a
        args.append(nc.dram_tensor(f"in_{name}_dram", a.shape, _mybir.dt.from_np(a.dtype),
                                   kind="ExternalInput").ap())
    args.append(nc.dram_tensor("out_0_dram", (1, S, D), F32, kind="ExternalOutput").ap())
    hybrid_block(nc, *args)
    r = _run(nc, [arrays], core_ids=[0])
    return r.results[0]["out_0_dram"]
```
